# Optimizing a Trainium2 kernel written in Bass

```python
import math
import jax, jax.numpy as jnp
from jax import lax
import numpy as np

D_MODEL = 1024
BATCH = 1
SEQ = 256
DEPTH = 1

CHUNK = 64
CONV_WIDTH = 1024
CONV_K = 3
SSM_WIDTH = 512
SSM_GROUP = 16
SSM_GROUPS = SSM_WIDTH // SSM_GROUP
SSM_STATE = 64
DT_MIN = 1e-3
DT_MAX = 1e-1
N_BRANCHES = 2
IN_COLS = 3 * CONV_WIDTH + SSM_WIDTH + N_BRANCHES * D_MODEL
N_EXPERT_GROUPS = 4
EXPERTS_PER_GROUP = 8
N_EXPERTS = N_EXPERT_GROUPS * EXPERTS_PER_GROUP
EXPERT_FF = 512
TOP_K_INNER = 2
EPS = 1e-6

kernel_name = "hybrid_conv_s5_hiermoe_block"

def rms_norm(x, g):
    xf = x.astype(jnp.float32)
    y = xf * lax.rsqrt(jnp.mean(xf * xf, axis=-1, keepdims=True) + EPS)
    return (y * g.astype(jnp.float32)).astype(x.dtype)

def short_conv_branch(xc, bg, cg, conv_w, conv_b, w_out):
    v = cg * xc
    y = lax.conv_general_dilated(
        v, conv_w.astype(v.dtype), window_strides=(1,), padding=[(CONV_K - 1, 0)],
        dimension_numbers=("NWC", "WIO", "NWC"), feature_group_count=CONV_WIDTH)
    y = y + conv_b
    return (bg * y) @ w_out

def _ssm_combine(e1, e2):
    a1, s1 = e1
    a2, s2 = e2
    return a1 * a2, a2 * s1 + s2

def s5_branch(u, a_re, a_im, log_dt, b_re, b_im, c_re, c_im, d_skip, w_glu_a, w_glu_b):
    bsz, length, _ = u.shape
    f32 = jnp.float32
    uf = u.astype(f32).reshape(bsz, length, SSM_GROUPS, SSM_GROUP)
    lam = lax.complex(a_re.astype(f32), a_im.astype(f32))
    dt = jnp.exp(log_dt.astype(f32))[:, None]
    a_bar = jnp.exp(lam * dt)
    b = lax.complex(b_re.astype(f32), b_im.astype(f32))
    b_bar = ((a_bar - 1.0) / lam)[..., None] * b
    bu = lax.complex(jnp.einsum("gnh,blgh->blgn", b_bar.real, uf),
                     jnp.einsum("gnh,blgh->blgn", b_bar.imag, uf))
    a_seq = jnp.broadcast_to(a_bar[None, None], bu.shape)
    _, states = lax.associative_scan(_ssm_combine, (a_seq, bu), axis=1)
    y = (jnp.einsum("ghn,blgn->blgh", c_re.astype(f32), states.real)
         - jnp.einsum("ghn,blgn->blgh", c_im.astype(f32), states.imag))
    y = y.reshape(bsz, length, SSM_WIDTH) + d_skip.astype(f32) * u.astype(f32)
    y = jax.nn.gelu(y).astype(u.dtype)
    return (y @ w_glu_a) * jax.nn.sigmoid(y @ w_glu_b)

def hier_moe(h, w_route_group, b_route_group, w_route_expert, b_route_expert,
             w_gate, w_up, w_down):
    bsz, length, d = h.shape
    t = bsz * length
    hf = h.reshape(t, d)
    f32 = jnp.float32
    pg = jax.nn.softmax((hf @ w_route_group + b_route_group).astype(f32), axis=-1)
    pg_top, g_idx = lax.top_k(pg, 1)
    le = (hf @ w_route_expert + b_route_expert).astype(f32).reshape(t, N_EXPERT_GROUPS, EXPERTS_PER_GROUP)
    le_sel = jnp.take_along_axis(le, g_idx[:, :, None], axis=1)[:, 0]
    pe = jax.nn.softmax(le_sel, axis=-1)
    pe_top, e_idx = lax.top_k(pe, TOP_K_INNER)
    pe_top = pe_top / jnp.sum(pe_top, axis=-1, keepdims=True)
    weights = pg_top * pe_top
    expert_ids = g_idx * EXPERTS_PER_GROUP + e_idx
    combine = jnp.sum(jax.nn.one_hot(expert_ids, N_EXPERTS, dtype=f32) * weights[..., None], axis=1)
    out = jnp.zeros((t, d), f32)
    for e in range(N_EXPERTS):
        a = jax.nn.silu(hf @ w_gate[e]) * (hf @ w_up[e])
        out = out + combine[:, e:e + 1] * (a @ w_down[e]).astype(f32)
    return out.astype(h.dtype).reshape(bsz, length, d)

def setup_inputs(seed: int = 0) -> dict:
    key = jax.random.key(seed)
    ks = jax.random.split(key, 24)
    f32 = jnp.float32
    nrm = lambda k, shape, scale: jax.random.normal(k, shape, f32) * scale
    L_, D = DEPTH, D_MODEL
    G, N, H = SSM_GROUPS, SSM_STATE, SSM_GROUP
    return {
        "x": nrm(ks[0], (BATCH, SEQ, D), 1.0),
        "norm_mix": 1.0 + nrm(ks[1], (L_, D), 0.01),
        "w_in": nrm(ks[2], (L_, D, IN_COLS), D ** -0.5),
        "conv_w": nrm(ks[3], (L_, CONV_K, 1, CONV_WIDTH), CONV_K ** -0.5),
        "conv_b": nrm(ks[4], (L_, CONV_WIDTH), 0.01),
        "w_conv_out": nrm(ks[5], (L_, CONV_WIDTH, D), CONV_WIDTH ** -0.5),
        "ssm_a_re": -0.5 + nrm(ks[6], (L_, G, N), 0.01),
        "ssm_a_im": jnp.pi * jnp.arange(N, dtype=f32)[None, None, :] + nrm(ks[7], (L_, G, N), 0.01),
        "ssm_log_dt": jax.random.uniform(ks[8], (L_, G), f32, math.log(DT_MIN), math.log(DT_MAX)),
        "ssm_b_re": nrm(ks[9], (L_, G, N, H), (2 * H) ** -0.5),
        "ssm_b_im": nrm(ks[10], (L_, G, N, H), (2 * H) ** -0.5),
        "ssm_c_re": nrm(ks[11], (L_, G, H, N), (2 * N) ** -0.5),
        "ssm_c_im": nrm(ks[12], (L_, G, H, N), (2 * N) ** -0.5),
        "ssm_d": nrm(ks[13], (L_, SSM_WIDTH), 1.0),
        "w_glu_a": nrm(ks[14], (L_, SSM_WIDTH, D), SSM_WIDTH ** -0.5),
        "w_glu_b": nrm(ks[15], (L_, SSM_WIDTH, D), SSM_WIDTH ** -0.5),
        "gate_bias": nrm(ks[16], (L_, N_BRANCHES, D), 0.01),
        "w_o": nrm(ks[17], (L_, D, D), D ** -0.5),
        "norm_ffn": 1.0 + nrm(ks[18], (L_, D), 0.01),
        "w_route_group": nrm(ks[19], (L_, D, N_EXPERT_GROUPS), D ** -0.5),
        "b_route_group": nrm(ks[20], (L_, N_EXPERT_GROUPS), 0.01),
        "w_route_expert": nrm(ks[21], (L_, D, N_EXPERTS), D ** -0.5),
        "b_route_expert": nrm(ks[22], (L_, N_EXPERTS), 0.01),
        "w_gate": nrm(jax.random.fold_in(ks[23], 0), (L_, N_EXPERTS, D, EXPERT_FF), D ** -0.5),
        "w_up": nrm(jax.random.fold_in(ks[23], 1), (L_, N_EXPERTS, D, EXPERT_FF), D ** -0.5),
        "w_down": nrm(jax.random.fold_in(ks[23], 2), (L_, N_EXPERTS, EXPERT_FF, D), EXPERT_FF ** -0.5),
        "norm_final": 1.0 + nrm(jax.random.fold_in(ks[23], 3), (D,), 0.01),
    }

def reference(x, norm_mix, w_in, conv_w, conv_b, w_conv_out, ssm_a_re, ssm_a_im, ssm_log_dt,
              ssm_b_re, ssm_b_im, ssm_c_re, ssm_c_im, ssm_d, w_glu_a, w_glu_b, gate_bias, w_o,
              norm_ffn, w_route_group, b_route_group, w_route_expert, b_route_expert,
              w_gate, w_up, w_down, norm_final):
    bsz, length, d = x.shape
    c0, c1, c2, c3 = CONV_WIDTH, 2 * CONV_WIDTH, 3 * CONV_WIDTH, 3 * CONV_WIDTH + SSM_WIDTH
    for l in range(DEPTH):
        h = rms_norm(x, norm_mix[l])
        p = h @ w_in[l]
        xc, bg, cg, u, gl = p[..., :c0], p[..., c0:c1], p[..., c1:c2], p[..., c2:c3], p[..., c3:]
        gates = jax.nn.sigmoid(gl.reshape(bsz, length, N_BRANCHES, d) + gate_bias[l])
        ya = short_conv_branch(xc, bg, cg, conv_w[l], conv_b[l], w_conv_out[l])
        yb = s5_branch(u, ssm_a_re[l], ssm_a_im[l], ssm_log_dt[l], ssm_b_re[l], ssm_b_im[l],
                       ssm_c_re[l], ssm_c_im[l], ssm_d[l], w_glu_a[l], w_glu_b[l])
        mixed = gates[..., 0, :] * ya + gates[..., 1, :] * yb
        x = x + mixed @ w_o[l]
        h2 = rms_norm(x, norm_ffn[l])
        x = x + hier_moe(h2, w_route_group[l], b_route_group[l], w_route_expert[l],
                         b_route_expert[l], w_gate[l], w_up[l], w_down[l])
    return rms_norm(x, norm_final)


_drawn_inputs = setup_inputs


def setup_inputs(seed=0):
    import zlib

    import numpy as np

    out = dict(_drawn_inputs(seed))
    spreads = {}
    factors = {'conv_b': 3.541,
     'ssm_a_re': 64.0,
     'ssm_log_dt': 16.452,
     'ssm_b_re': 25.32,
     'ssm_b_im': 17.075,
     'ssm_c_im': 12.059,
     'gate_bias': 8.0,
     'norm_ffn': 2.712,
     'b_route_group': 3.612,
     'b_route_expert': 8.0,
     'norm_final': 34.49,
     'ssm_a_im': 4.196,
     'ssm_c_re': 8.0}
    for name, (base, spread) in spreads.items():
        noise = np.random.default_rng([zlib.crc32(name.encode()), seed]).standard_normal(out[name].shape)
        drawn = base * np.exp(spread * noise) if base else spread * noise
        out[name] = __import__('jax').numpy.asarray(drawn.astype(out[name].dtype))
    for name, factor in factors.items():
        out[name] = (out[name] * factor).astype(out[name].dtype)
    return out
```

```python
from contextlib import ExitStack

import concourse.bass as bass
from concourse import mybir

D = 1024
T = 256
P = 128
KD = D // P
TB = T // P
SSM = 512
YB = SSM // P
GROUPS, STATE, GH = 32, 64, 16
ST = GROUPS * STATE // P
NEG, EG, NE = 4, 8, 32
FF = 512
KF = FF // P
EPS = 1e-6

UNIT = 4096
RING = 8
MIX_UNITS = 17
SLOTS = 32
PACK = P // SLOTS
PACKS = NE // PACK
PACK_UNITS = 12
ROUND_UNITS = PACKS * PACK_UNITS
BODY_PACKS = 2
BODY_UNITS = BODY_PACKS * PACK_UNITS
BODIES = PACKS // BODY_PACKS
ROUNDS = T // SLOTS
UNSELECTED = 1.0e4

TWO_PI = 6.283185307179586
PI_HI, PI_MID = 6.28125, 0.0019350051879882812
PI_LO = TWO_PI - PI_HI - PI_MID
ROUNDER = 12582912.0
PI_CLAMP = 3.1415925
EULER = 2.718281828459045
MASKED = -1.0e30

R_GMIX, R_CONVW, R_CONVB, R_GATEB, R_SSMD, R_ARE, R_AIM, N_ROWS = 0, 8, 32, 40, 56, 60, 76, 92

EVEN_BANKS, ODD_BANKS = (0, 1, 4, 5), (2, 3, 6, 7)

N_MAIN = 48
S5_LAG = 2


def mixer_schedule():
    order, step = [], 0
    for g in range(N_MAIN):
        order.append(("main", g))
        if g >= 4 and g % 2 == 0 and step < ST + S5_LAG:
            order.append(("s5", step))
            step += 1
    while step < ST + S5_LAG:
        order.append(("s5", step))
        step += 1
    return order


def block_kernel(nc, x_in, norm_mix, w_in, conv_w, conv_b, w_conv_out, a_re, a_im, log_dt, b_re, b_im,
                 c_re, c_im, ssm_d, w_glu_a, w_glu_b, gate_bias, w_o, norm_ffn, w_rg, b_rg, w_re, b_re_,
                 w_gate, w_up, w_down, norm_final, out):
    f32 = mybir.dt.float32
    i32 = mybir.dt.int32
    ALU = mybir.AluOpType
    ACT = mybir.ActivationFunctionType
    AX = mybir.AxisListType
    SCHEDULE = mixer_schedule()

    ctx = ExitStack()
    with ctx:
        def sb(name, shape, dt=f32):
            return ctx.enter_context(nc.sbuf_tensor(name, shape, dt))

        def sem(name):
            return ctx.enter_context(nc.semaphore(name))

        ring = sb("ring", [P, RING, UNIT])
        hT = sb("hT", [P, KD, T])
        mixed = sb("mixed", [P, KD, T])
        rows = sb("rows", [N_ROWS, P])
        cols = sb("cols", [P, 128])
        logdt_row = sb("logdt_row", [1, GROUPS])
        ident = sb("ident", [P, P])
        ones = sb("ones", [P, P])
        upper = sb("upper", [P, P])
        s5c = sb("s5c", [P, 16, ST])
        dt_t = sb("dt_t", [P, ST])
        eul = sb("eul", [P, ST])
        par_i = sb("par_i", [P, 1], i32)
        par = sb("par", [P, 2])
        zeros = sb("zeros", [P, 512], mybir.dt.bfloat16)
        lowT = sb("lowT", [P, 2, ST, 16])
        highT = sb("highT", [P, 2, ST, 16])
        ptmp = sb("ptmp", [P, 2, ST, 8])
        xs = sb("xs", [P, 2, T])
        v_sb = sb("v_sb", [P, 2, T + 2])
        ct = sb("ct", [P, 2, T])
        gate = sb("gate", [P, 2, T])
        stat = sb("stat", [P, 12])
        halfneg = sb("halfneg", [P, 2])
        wr = sb("wr", [P, KD, NEG + NE])
        br = sb("br", [P, NEG + NE])
        rs = sb("rs", [P, 16, TB])
        iota = sb("iota", [P, NE])
        slot_no = sb("slot_no", [P, SLOTS])
        cnt_f = sb("cnt_f", [P, 1])
        most = sb("most", [P, 1], i32)

        def region(name, n):
            flat = sb(name, [P, n])

            def view(at, *shape):
                size = 1
                for d in shape:
                    size *= d
                assert at + size <= n
                names = "abcd"[:len(shape)]
                form = f"p ({' '.join(names)}) -> p {' '.join(names)}"
                return flat[:, at:at + size].rearrange(form, **dict(zip(names, shape)))
            return view

        x_region = region("x_region", TB * D)
        x_sb = x_region(0, TB, D)
        rtmp = x_region(0, 4, T)
        turned = x_region(4 * T, 2, 2, T)
        h2_region = region("h2_region", TB * D)
        zb = h2_region(0, 2, ST, 2 * GH)
        zc = h2_region(D, 2, YB, 2, STATE)
        q_sb = h2_region(0, 2, 2, 2, T)
        h2 = h2_region(0, TB, KD, P)
        z_region = region("z_region", KD * T)
        bld = z_region(0, 2, ST, GH)
        btmp = z_region(512, 4, ST, GH)
        cld = z_region(1536, 2, YB, STATE)
        z_sb = z_region(0, KD, T)
        u_region = region("u_region", D)
        uT = u_region(0, YB, T)
        g_ffn = u_region(0, D)
        y_region = region("y_region", D)
        yT = y_region(0, YB, T)
        g_fin = y_region(0, D)
        bt_region = region("bt_region", YB * 2 * P)
        BT = bt_region(0, YB, 2, P)
        rt = bt_region(0, TB, 12, NE)
        ct_region = region("ct_region", 2 * YB * P)
        CT = ct_region(0, 2, YB, P)
        sel = ct_region(0, TB, PACK, SLOTS)
        wsel = ct_region(256, TB, PACK, SLOTS)
        member = ct_region(512, TB, NE)
        weight = ct_region(576, TB, NE)
        rank = ct_region(640, TB, NE)
        wselT = ct_region(704, TB, P)
        rot_region = region("rot_region", 4 * D)
        rot = rot_region(0, 2, 2, 4, T)
        xT = rot_region(0, KD, P)
        silu = rot_region(1024, FF)
        act_sb = rot_region(1536, KF, P)
        actT = rot_region(2048, KF, P)
        y_sb = rot_region(2560, D)
        sq = y_sb

        bank = [ctx.enter_context(nc.psum_tensor(f"bank{i}", [P, 512], f32)) for i in range(8)]

        loaded = [sem(f"loaded{i}") for i in range(RING)]
        units_used = sem("units_used")
        x_in_s = [sem(f"x_in{i}") for i in range(TB)]
        rows_in = sem("rows_in")
        b_in = sem("b_in")
        c_in = sem("c_in")
        route_in = sem("route_in")
        ffn_in = sem("ffn_in")
        fin_in = sem("fin_in")
        consts = sem("consts")
        pool_step = sem("pool_step")
        act_step = sem("act_step")
        dve_step = sem("dve_step")
        sumsq = sem("sumsq")
        meansq = sem("meansq")
        rstd = sem("rstd")
        xn_ready = sem("xn_ready")
        cols_psum = sem("cols_psum")
        cols_ready = sem("cols_ready")
        dt_ready = sem("dt_ready")
        hT_psum = sem("hT_psum")
        hT_act = sem("hT_act")
        hT_dve = sem("hT_dve")
        u_psum = sem("u_psum")
        u_ready = sem("u_ready")
        expo_ready = sem("expo_ready")
        rho_ready = sem("rho_ready")
        angle_ready = sem("angle_ready")
        sines_ready = sem("sines_ready")
        zb_ready = sem("zb_ready")
        zc_ready = sem("zc_ready")
        bt_psum = sem("bt_psum")
        bt_ready = sem("bt_ready")
        ct_ready = sem("ct_ready")
        powers_ready = sem("powers_ready")
        rot_ready = sem("rot_ready")
        rot_used = sem("rot_used")
        bu_psum = sem("bu_psum")
        bu_used = sem("bu_used")
        q_ready = sem("q_ready")
        s_ready = sem("s_ready")
        q_used = sem("q_used")
        ypre_ready = sem("ypre_ready")
        y_ready = sem("y_ready")
        xbc_psum = sem("xbc_psum")
        xs_ready = sem("xs_ready")
        z_ready = sem("z_ready")
        ya_psum = sem("ya_psum")
        ya_ready = sem("ya_ready")
        ga_psum = sem("ga_psum")
        ga_ready = sem("ga_ready")
        ga_used = sem("ga_used")
        gb_psum = sem("gb_psum")
        gb_ready = sem("gb_ready")
        glu_psum = sem("glu_psum")
        glu_sig = sem("glu_sig")
        mixed_ready = sem("mixed_ready")
        wo_psum = sem("wo_psum")
        x2_ready = sem("x2_ready")
        h2_ready = sem("h2_ready")
        h2T_psum = sem("h2T_psum")
        logits_psum = sem("logits_psum")
        expin_ready = sem("expin_ready")
        exp_ready = sem("exp_ready")
        member_ready = sem("member_ready")
        rank_psum = sem("rank_psum")
        most_ready = sem("most_ready")
        sel_ready = sem("sel_ready")
        wsel_ready = sem("wsel_ready")
        gather_psum = sem("gather_psum")
        wselT_psum = sem("wselT_psum")
        wselT_ready = sem("wselT_ready")
        xT_act = sem("xT_act")
        xT_dve = sem("xT_dve")
        up_psum = sem("up_psum")
        silu_ready = sem("silu_ready")
        act_ready = sem("act_ready")
        actT_psum = sem("actT_psum")
        actT_ready = sem("actT_ready")
        down_psum = sem("down_psum")
        y_act = sem("y_act")
        y_dve = sem("y_dve")
        slots_moved = sem("slots_moved")
        moe_psum = sem("moe_psum")
        out_ready = sem("out_ready")
        stored = sem("stored")

        def mix_slot(u):
            return ring[:, u % RING, :]

        def mix_loaded(eng, u):
            eng.wait_ge(loaded[u % RING], 16 * (u // RING + 1))

        def w8(u):
            return mix_slot(u).rearrange("p (k n) -> p k n", k=KD)

        def w4(u):
            return mix_slot(u).rearrange("p (k n) -> p k n", k=4)

        U_U, U_XBC, U_CO, U_GA, U_GB, U_GLUB, U_GLUA, U_WO = 0, 1, 7, 9, 11, 13, 14, 15

        def psum_half(i):
            return bank[i // 2][:, (i % 2) * T:(i % 2) * T + T]

        block = ctx.enter_context(nc.Block())

        @block.sync
        def _(sp):
            def in_cols(c0):
                return w_in[0].rearrange("(k p) n -> p k n", p=P)[:, :, c0:c0 + 512]

            xbc = [in_cols(part * D + half * 512) for half in range(2) for part in range(3)]
            co = w_conv_out[0].rearrange("(k p) n -> p k n", p=P)
            wo = w_o[0].rearrange("(k p) n -> p k n", p=P)
            sources = [in_cols(3 * D)] + xbc + [co[:, :, 0:512], co[:, :, 512:D]]
            sources += [in_cols(3 * D + SSM + i * 512) for i in range(4)]
            sources += [w_glu_b[0].rearrange("(k p) n -> p k n", p=P), w_glu_a[0].rearrange("(k p) n -> p k n", p=P)]
            sources += [wo[:, 0:4, :], wo[:, 4:8, :]]
            assert len(sources) == MIX_UNITS
            for r, n, src in ((R_GMIX, KD, norm_mix[0]), (R_CONVW, 3 * KD, conv_w[0].rearrange("a b c -> (a b c)")),
                              (R_CONVB, KD, conv_b[0]), (R_GATEB, 2 * KD, gate_bias[0].rearrange("a c -> (a c)")),
                              (R_SSMD, YB, ssm_d[0]), (R_ARE, ST, a_re[0].rearrange("g n -> (g n)")),
                              (R_AIM, ST, a_im[0].rearrange("g n -> (g n)"))):
                sp.dma_start(rows[r:r + n, :], src.rearrange("(r c) -> r c", c=P)).then_inc(rows_in, 16)
            sp.dma_start(logdt_row[:], log_dt[0:1, :]).then_inc(rows_in, 16)
            for u, src in enumerate(sources):
                if u == 1:
                    for i, part in enumerate((b_re, b_im)):
                        sp.dma_start(bld[:, i], part[0].rearrange("(t g) n h -> (g n) t h", g=2)).then_inc(b_in, 16)
                    for i, part in enumerate((c_re, c_im)):
                        sp.dma_start(cld[:, i], part[0].rearrange("(b g) h n -> (g h) b n", g=8)).then_inc(c_in, 16)
                if u == 5:
                    sp.dma_start(wr[:, :, 0:NEG], w_rg[0].rearrange("(p k) n -> p k n", p=P)).then_inc(route_in, 16)
                    sp.dma_start(wr[:, :, NEG:], w_re[0].rearrange("(p k) n -> p k n", p=P)).then_inc(route_in, 16)
                    sp.dma_start(br[:, 0:NEG], b_rg.to_broadcast([P, NEG])).then_inc(route_in, 16)
                    sp.dma_start(br[:, NEG:], b_re_.to_broadcast([P, NE])).then_inc(route_in, 16)
                if u >= RING:
                    sp.wait_ge(units_used, u - RING + 1)
                sp.dma_start(mix_slot(u).rearrange("p (k n) -> p k n", k=src.shape[1]), src).then_inc(loaded[u % RING], 16)

            gate_v = w_gate[0].rearrange("e (p k) n -> p e (k n)", p=P)
            up_v = w_up[0].rearrange("e (p k) n -> p e (k n)", p=P)
            down_v = w_down[0].rearrange("e (p c) n -> p e (c n)", p=P)

            def load_round(used_base):
                with sp.Fori(0, BODIES) as it:
                    for v in range(BODY_UNITS):
                        pk, w = v // PACK_UNITS, v % PACK_UNITS
                        slot = (MIX_UNITS + v) % RING
                        first = it * (BODY_PACKS * PACK) + pk * PACK
                        sp.wait_ge(units_used, used_base + it * BODY_UNITS + (v + MIX_UNITS - RING + 1))
                        if w < 8:
                            view = gate_v if w % 2 == 0 else up_v
                            src = view[:, bass.ds(first, PACK), (w // 2) * 1024:(w // 2 + 1) * 1024]
                        else:
                            src = down_v[:, bass.ds(first, PACK), (w - 8) * D:(w - 7) * D]
                        sp.dma_start(ring[:, slot, :].rearrange("p (e n) -> p e n", e=PACK), src)\
                            .then_inc(loaded[slot], 16)

            load_round(0)
            sp.wait_ge(most_ready, 1)
            most_r = sp.value_load(most[0:1, 0:1], min_val=0, max_val=T)
            with sp.Fori(1, ROUNDS) as rnd:
                with sp.If(most_r > rnd * SLOTS):
                    load_round(rnd * ROUND_UNITS)
            for b in range(TB):
                sp.wait_ge(out_ready, b + 1)
                sp.dma_start(out[0, b * P:(b + 1) * P, :], x_sb[:, b, :]).then_inc(stored, 16)
            sp.wait_ge(stored, 16 * TB)

        @block.gpsimd
        def _(pool):
            steps = [0]

            def link(ins):
                steps[0] += 1
                ins.then_inc(pool_step, 1)
                pool.wait_ge(pool_step, steps[0])

            nc.gpsimd.memset(halfneg[:], -0.5)
            nc.gpsimd.memset(eul[:], EULER)
            nc.gpsimd.memset(zeros[:], 0.0)
            nc.gpsimd.memset(ones[:], 1.0)
            nc.gpsimd.memset(zb, 0.0)
            nc.gpsimd.memset(v_sb[:], 0.0)
            nc.gpsimd.memset(lowT[:, 1], 0.0)
            nc.gpsimd.memset(highT[:, 1], 0.0)
            nc.gpsimd.memset(lowT[:, 0], 1.0)
            nc.gpsimd.memset(highT[:, 0], 1.0)
            link(nc.gpsimd.memset(ident[:], 0.0))
            nc.gpsimd.affine_select(out=ident[:], in_=ident[:], compare_op=ALU.not_equal, fill=1.0, base=0,
                                    pattern=[[-1, P]], channel_multiplier=1).then_inc(consts, 1)
            nc.gpsimd.affine_select(out=upper[:], in_=ones[:], compare_op=ALU.is_gt, fill=0.0, base=0,
                                    pattern=[[1, P]], channel_multiplier=-1)
            nc.gpsimd.iota(iota[:], pattern=[[1, NE]], base=0, channel_multiplier=0,
                           allow_small_or_imprecise_dtypes=True)
            nc.gpsimd.iota(slot_no[:], pattern=[[1, SLOTS]], base=0, channel_multiplier=0,
                           allow_small_or_imprecise_dtypes=True).then_inc(slots_moved, 1)
            nc.gpsimd.iota(par_i[:], pattern=[[0, 1]], base=0, channel_multiplier=1).then_inc(consts, 1)
            pool.wait_ge(meansq, 1)
            nc.gpsimd.tensor_tensor(stat[:, 4:6], stat[:, 2:4], halfneg[:], ALU.pow).then_inc(rstd, 1)
            pool.wait_ge(cols_ready, 2)
            nc.gpsimd.tensor_tensor(dt_t[:], eul[:], s5c[:, 0, :], ALU.pow).then_inc(dt_ready, 1)
            pool.wait_ge(expo_ready, 1)
            nc.gpsimd.tensor_tensor(s5c[:, 2, :], eul[:], s5c[:, 1, :], ALU.pow).then_inc(rho_ready, 1)
            pool.wait_ge(powers_ready, 1)

            def rotations(b):
                if b >= 2:
                    pool.wait_ge(rot_used, b - 1)
                lo = [lowT[:, i, 4 * b:4 * b + 4, :].unsqueeze(2).to_broadcast([P, 4, 16, 16]) for i in range(2)]
                hi = [highT[:, i, 4 * b:4 * b + 4, :].unsqueeze(3).to_broadcast([P, 4, 16, 16]) for i in range(2)]
                o = [rot[:, b % 2, i].rearrange("p t (h l) -> p t h l", l=16) for i in range(2)]
                tmp = rtmp.rearrange("p t (h l) -> p t h l", l=16)
                nc.gpsimd.tensor_tensor(o[0], lo[0], hi[0], ALU.mult)
                link(nc.gpsimd.tensor_tensor(tmp, lo[1], hi[1], ALU.mult))
                link(nc.gpsimd.tensor_tensor(o[0], o[0], tmp, ALU.subtract))
                nc.gpsimd.tensor_tensor(o[1], lo[0], hi[1], ALU.mult)
                link(nc.gpsimd.tensor_tensor(tmp, lo[1], hi[0], ALU.mult))
                nc.gpsimd.tensor_tensor(o[1], o[1], tmp, ALU.add).then_inc(rot_ready, 1)
                pool.wait_ge(rot_ready, b + 1)

            def state_sums(t):
                q = q_sb[:, t % 2]
                pool.wait_ge(q_ready, t + 1)
                nc.gpsimd.tensor_tensor(q[:, 0, 0, :], q[:, 0, 0, :], q[:, 1, 1, :], ALU.subtract)
                nc.gpsimd.tensor_tensor(q[:, 0, 1, :], q[:, 0, 1, :], q[:, 1, 0, :], ALU.add).then_inc(s_ready, 1)

            rotations(0)
            rotations(1)
            for t in range(ST):
                state_sums(t)
                if t % 4 == 3 and t // 4 + 2 < YB:
                    rotations(t // 4 + 2)
            for n in range(2):
                pool.wait_ge(meansq, 2 + n)
                nc.gpsimd.tensor_tensor(stat[:, 4:6], stat[:, 2:4], halfneg[:], ALU.pow).then_inc(rstd, 1)

        @block.scalar
        def _(act):
            steps = [0]

            def link(ins):
                steps[0] += 1
                ins.then_inc(act_step, 1)
                act.wait_ge(act_step, steps[0])

            for b in range(TB):
                act.dma_start(x_sb[:, b, :], x_in[0, b * P:(b + 1) * P, :]).then_inc(x_in_s[b], 16)

            for b in range(TB):
                act.wait_ge(x_in_s[b], 16)
                if b:
                    act.wait_ge(sumsq, b)
                nc.scalar.activation(sq, x_sb[:, b, :], ACT.Square, accum_out=stat[:, b:b + 1]).then_inc(sumsq, 1)
            act.wait_ge(cols_psum, 1)
            nc.scalar.activation(cols[:, 0:N_ROWS], bank[0][:, 0:N_ROWS], ACT.Copy).then_inc(cols_ready, 1)
            for g in range(2):
                ins = nc.scalar.activation(s5c[64 * g:64 * g + 64, 0, :],
                                           bank[0][64 * g:64 * g + 64, 128 + g:128 + GROUPS:2], ACT.Copy)
            ins.then_inc(cols_ready, 1)
            act.wait_ge(cols_ready, 2)
            for k in EVEN_BANKS:
                act.wait_ge(hT_psum, k - k % 2 + 2)
                nc.scalar.activation(hT[:, k, :], psum_half(8 + k), ACT.Copy,
                                     scale=cols[:, R_GMIX + k:R_GMIX + k + 1]).then_inc(hT_act, 1)
            act.wait_ge(angle_ready, 1)
            nc.scalar.activation(s5c[:, 5, :], s5c[:, 4, :], ACT.Sin)
            nc.scalar.activation(s5c[:, 6, :], s5c[:, 4, :], ACT.Sin, scale=0.5).then_inc(sines_ready, 1)
            for n in range(YB):
                act.wait_ge(u_psum, n - n % 2 + 2)
                nc.scalar.activation(uT[:, n, :], psum_half(4 + n), ACT.Copy).then_inc(u_ready, 1)
            act.wait_ge(bt_psum, 1)
            for i in range(2):
                ins = nc.scalar.activation(BT[:, :, i, :], bank[4 + i][:].rearrange("p (b n) -> p b n", b=YB), ACT.Copy)
            ins.then_inc(bt_ready, 1)

            def main(g):
                if g < 24:
                    j = g // 3
                    if g % 3 == 0:
                        act.wait_ge(xbc_psum, g + 1)
                        if j >= 2:
                            act.wait_ge(z_ready, j - 1)
                        nc.scalar.activation(xs[:, j % 2, :], bank[2 * (j % 2)][:, 0:T], ACT.Copy).then_inc(xs_ready, 1)
                elif g < 32:
                    n = g - 24
                    act.wait_ge(ya_psum, n + 1)
                    nc.scalar.activation(mixed[:, n, :], bank[n % 4][:, 0:T], ACT.Copy).then_inc(ya_ready, 1)
                elif g < 40:
                    n = g - 32
                    act.wait_ge(ga_psum, n + 1)
                    if n >= 2:
                        act.wait_ge(ga_used, n - 1)
                    nc.scalar.activation(gate[:, n % 2, :], bank[n % 4][:, 0:T], ACT.Sigmoid,
                                         bias=cols[:, R_GATEB + n:R_GATEB + n + 1]).then_inc(ga_ready, 1)
                else:
                    n = g - 40
                    act.wait_ge(gb_psum, n + 1)
                    nc.scalar.activation(z_sb[:, n, :], bank[n % 4][:, 0:T], ACT.Sigmoid,
                                         bias=cols[:, R_GATEB + KD + n:R_GATEB + KD + n + 1]).then_inc(gb_ready, 1)

            def s5(t):
                if t >= 6 and (t - 6) % 4 == 0:
                    gelu((t - 6) // 4)

            def gelu(b):
                act.wait_ge(ypre_ready, b + 1)
                nc.scalar.activation(yT[:, b, :], yT[:, b, :], ACT.Gelu_apprx_tanh).then_inc(y_ready, 1)

            for what, n in SCHEDULE:
                main(n) if what == "main" else s5(n)
            act.wait_ge(s_ready, ST)
            act.wait_ge(rot_ready, YB)
            for b in range(TB):
                act.dma_start(x_sb[:, b, :], x_in[0, b * P:(b + 1) * P, :]).then_inc(x_in_s[b], 16)
            gelu(YB - 1)
            act.dma_start(g_ffn, norm_ffn.to_broadcast([P, D])).then_inc(ffn_in, 16)
            for n in range(KD):
                act.wait_ge(glu_psum, 2 * n + 1)
                if n >= 2:
                    act.wait_ge(mixed_ready, n - 1)
                nc.scalar.activation(gate[:, n % 2, :], bank[2 * (n % 2)][:, 0:T], ACT.Sigmoid).then_inc(glu_sig, 1)
            act.wait_ge(glu_psum, 2 * KD)
            act.dma_start(g_fin, norm_final.unsqueeze(0).to_broadcast([P, D])).then_inc(fin_in, 16)
            for b in range(TB):
                act.wait_ge(x2_ready, 2 * (b + 1))
                act.wait_ge(sumsq, 2 + b)
                nc.scalar.activation(sq, x_sb[:, b, :], ACT.Square, accum_out=stat[:, b:b + 1]).then_inc(sumsq, 1)
            for k in EVEN_BANKS:
                act.wait_ge(h2T_psum, k - k % 2 + 2)
                nc.scalar.activation(hT[:, k, :], psum_half(8 + k), ACT.Copy).then_inc(hT_act, 1)
            for n in range(2):
                act.wait_ge(expin_ready, n + 1)
                if n == 0:
                    ins = nc.scalar.activation(rt[:, :, 1, 0:NEG], rt[:, :, 0, 0:NEG], ACT.Exp)
                else:
                    ins = nc.scalar.activation(rs[:, 9, :], rs[:, 8, :], ACT.Exp)
                ins.then_inc(exp_ready, 1)

            act.wait_ge(most_ready, 1)
            most_r = act.value_load(most[0:1, 0:1], min_val=0, max_val=T)
            with act.Fori(0, ROUNDS) as rnd:
                with act.If(most_r > rnd * SLOTS):
                    with act.Fori(0, BODIES) as it:
                        for pk in range(BODY_PACKS):
                            done = rnd * PACKS + it * BODY_PACKS + (pk + 1)
                            act.wait_ge(gather_psum, done)
                            nc.scalar.activation(xT[:, 0:4, :], bank[6][:].rearrange("p (k s) -> p k s", k=4),
                                                 ACT.Copy).then_inc(xT_act, 1)
                            act.wait_ge(wselT_psum, done)
                            nc.scalar.activation(wselT, bank[5][:, 0:TB * P].rearrange("p (b t) -> p b t", b=TB),
                                                 ACT.Copy).then_inc(wselT_ready, 1)
                            act.wait_ge(up_psum, done)
                            nc.scalar.activation(silu, bank[4][:], ACT.Silu).then_inc(silu_ready, 1)
                            act.wait_ge(actT_psum, done)
                            nc.scalar.activation(actT, bank[4][:].rearrange("p (c s) -> p c s", c=KF),
                                                 ACT.Copy).then_inc(actT_ready, 1)
                            act.wait_ge(down_psum, done)
                            nc.scalar.activation(y_sb[:, 0:512], bank[6][:], ACT.Copy).then_inc(y_act, 1)
            act.wait_ge(moe_psum, 1)
            for b in range(TB):
                act.wait_ge(sumsq, 4 + 2 * b)
                for h in range(2):
                    nc.scalar.activation(h2[:, b, 4 * h:4 * h + 4, :].rearrange("p k n -> p (k n)"), bank[2 * b + h][:],
                                         ACT.Square, accum_out=stat[:, 6 + 2 * b + h:7 + 2 * b + h]).then_inc(sumsq, 1)

        @block.vector
        def _(dve):
            steps = [0]

            def link(ins):
                steps[0] += 1
                ins.then_inc(dve_step, 1)
                dve.wait_ge(dve_step, steps[0])

            V = nc.vector

            def mean_square():
                V.tensor_scalar(stat[:, 2:4], stat[:, 0:2], 1.0 / D, EPS, ALU.mult, ALU.add).then_inc(meansq, 1)

            dve.wait_ge(sumsq, 2)
            mean_square()
            dve.wait_ge(rstd, 1)
            xn = mixed[:].rearrange("p k t -> p (k t)").rearrange("p (b d) -> p b d", b=TB)
            for b in range(TB):
                V.tensor_scalar(xn[:, b, :], x_sb[:, b, :], stat[:, 4 + b:5 + b], None, ALU.mult).then_inc(xn_ready, 1)
            dve.wait_ge(cols_ready, 2)
            dve.wait_ge(dt_ready, 1)
            are, aim = cols[:, R_ARE:R_ARE + ST], cols[:, R_AIM:R_AIM + ST]

            def c(i):
                return s5c[:, i, :]

            V.tensor_tensor(c(1), are, dt_t[:], ALU.mult).then_inc(expo_ready, 1)
            link(V.tensor_tensor(c(3), aim, dt_t[:], ALU.mult))
            link(V.tensor_scalar(c(7), c(3), 1.0 / TWO_PI, ROUNDER, ALU.mult, ALU.add))
            link(V.tensor_scalar(c(7), c(7), ROUNDER, None, ALU.subtract))
            for part in (PI_HI, PI_MID, PI_LO):
                link(V.scalar_tensor_tensor(c(3), c(7), -part, c(3), ALU.mult, ALU.add))
            V.tensor_scalar(c(4), c(3), PI_CLAMP, -PI_CLAMP, ALU.min, ALU.max).then_inc(angle_ready, 1)
            for k in ODD_BANKS:
                dve.wait_ge(hT_psum, k - k % 2 + 2)
                V.tensor_scalar(hT[:, k, :], psum_half(8 + k), cols[:, R_GMIX + k:R_GMIX + k + 1], None, ALU.mult)\
                    .then_inc(hT_dve, 1)
            dve.wait_ge(consts, 2)
            link(V.tensor_scalar(par_i[:], par_i[:], 4, 1, ALU.logical_shift_right, ALU.bitwise_and))
            link(V.tensor_copy(par[:, 1:2], par_i[:]))
            link(V.tensor_scalar(par[:, 0:1], par[:, 1:2], -1.0, 1.0, ALU.mult, ALU.add))
            dve.wait_ge(c_in, 32)
            for i in range(2):
                for g in range(2):
                    ins = V.tensor_scalar(zc[:, i, :, g, :], cld[:, i], par[:, g:g + 1], None, ALU.mult)
            ins.then_inc(zc_ready, 1)
            link(V.tensor_tensor(c(8), are, are, ALU.mult))
            link(V.tensor_tensor(c(9), aim, aim, ALU.mult))
            link(V.tensor_tensor(c(8), c(8), c(9), ALU.add))
            link(V.reciprocal(c(9), c(8)))
            dve.wait_ge(sines_ready, 1)
            link(V.tensor_tensor(c(6), c(6), c(6), ALU.mult))
            link(V.tensor_scalar(c(6), c(6), -2.0, 1.0, ALU.mult, ALU.add))
            dve.wait_ge(rho_ready, 1)
            link(V.tensor_tensor(c(10), c(2), c(6), ALU.mult))
            link(V.tensor_scalar(c(10), c(10), 1.0, None, ALU.subtract))
            link(V.tensor_tensor(c(11), c(2), c(5), ALU.mult))
            V.tensor_tensor(c(12), c(10), are, ALU.mult)
            link(V.tensor_tensor(c(13), c(11), aim, ALU.mult))
            link(V.tensor_tensor(c(12), c(12), c(13), ALU.add))
            link(V.tensor_tensor(c(14), c(12), c(9), ALU.mult))
            V.tensor_tensor(c(12), c(11), are, ALU.mult)
            link(V.tensor_tensor(c(13), c(10), aim, ALU.mult))
            link(V.tensor_tensor(c(12), c(12), c(13), ALU.subtract))
            link(V.tensor_tensor(c(15), c(12), c(9), ALU.mult))
            dve.wait_ge(b_in, 32)
            kr = c(14).unsqueeze(2).to_broadcast([P, ST, GH])
            ki = c(15).unsqueeze(2).to_broadcast([P, ST, GH])
            V.tensor_tensor(btmp[:, 0], bld[:, 0], kr, ALU.mult)
            V.tensor_tensor(btmp[:, 1], bld[:, 1], ki, ALU.mult)
            V.tensor_tensor(btmp[:, 2], bld[:, 1], kr, ALU.mult)
            link(V.tensor_tensor(btmp[:, 3], bld[:, 0], ki, ALU.mult))
            for g in range(2):
                h = slice(64 * g, 64 * g + 64)
                V.tensor_tensor(zb[h, 0, :, GH * g:GH * g + GH], btmp[h, 0], btmp[h, 1], ALU.subtract)
                ins = V.tensor_tensor(zb[h, 1, :, GH * g:GH * g + GH], btmp[h, 2], btmp[h, 3], ALU.add)
            ins.then_inc(zb_ready, 1)

            def power(i, k, tbl):
                return tbl[:, i, :, k:k + 1]

            for tbl, first in ((lowT, None), (highT, lowT)):
                if first is None:
                    V.tensor_copy(power(0, 1, tbl), c(6).unsqueeze(2))
                    link(V.tensor_copy(power(1, 1, tbl), c(5).unsqueeze(2)))
                else:
                    r8, i8 = power(0, 8, first), power(1, 8, first)
                    V.tensor_tensor(ptmp[:, 0, :, 0:1], r8, r8, ALU.mult)
                    V.tensor_tensor(ptmp[:, 1, :, 0:1], i8, i8, ALU.mult)
                    link(V.scalar_tensor_tensor(power(1, 1, tbl), r8, 2.0, i8, ALU.mult, ALU.mult))
                    link(V.tensor_tensor(power(0, 1, tbl), ptmp[:, 0, :, 0:1], ptmp[:, 1, :, 0:1], ALU.subtract))
                n = 1
                while n < 16:
                    if n > 1:
                        r, i = power(0, n // 2, tbl), power(1, n // 2, tbl)
                        V.tensor_tensor(ptmp[:, 0, :, 0:1], r, r, ALU.mult)
                        V.tensor_tensor(ptmp[:, 1, :, 0:1], i, i, ALU.mult)
                        link(V.scalar_tensor_tensor(power(1, n, tbl), r, 2.0, i, ALU.mult, ALU.mult))
                        link(V.tensor_tensor(power(0, n, tbl), ptmp[:, 0, :, 0:1], ptmp[:, 1, :, 0:1], ALU.subtract))
                        m = n - 1
                        lo_r, lo_i = tbl[:, 0, :, 1:n], tbl[:, 1, :, 1:n]
                        pr = power(0, n, tbl).to_broadcast([P, ST, m])
                        pi = power(1, n, tbl).to_broadcast([P, ST, m])
                        t0, t1 = ptmp[:, 0, :, 0:m], ptmp[:, 1, :, 0:m]
                        V.tensor_tensor(t0, lo_r, pr, ALU.mult)
                        link(V.tensor_tensor(t1, lo_i, pi, ALU.mult))
                        link(V.tensor_tensor(tbl[:, 0, :, n + 1:2 * n], t0, t1, ALU.subtract))
                        V.tensor_tensor(t0, lo_r, pi, ALU.mult)
                        link(V.tensor_tensor(t1, lo_i, pr, ALU.mult))
                        link(V.tensor_tensor(tbl[:, 1, :, n + 1:2 * n], t0, t1, ALU.add))
                    n *= 2
            V.tensor_copy(par[:, 0:1], par[:, 1:2]).then_inc(powers_ready, 1)
            dve.wait_ge(bt_psum, 2)
            for i, (src, scale) in enumerate(((6, 1.0), (7, -1.0))):
                ins = V.tensor_scalar(CT[:, i], bank[src][:].rearrange("p (b n) -> p b n", b=YB), scale, None, ALU.mult)
            ins.then_inc(ct_ready, 1)

            def conv(j):
                s = j % 2
                w = [cols[:, R_CONVW + KD * i + j:R_CONVW + KD * i + j + 1] for i in range(3)]
                dve.wait_ge(xs_ready, j + 1)
                dve.wait_ge(xbc_psum, 3 * j + 3)
                link(V.tensor_tensor(v_sb[:, s, 2:T + 2], bank[2 * s + 1][:, T:2 * T], xs[:, s, :], ALU.mult))
                link(V.tensor_scalar(ct[:, 0, :], v_sb[:, s, 2:T + 2], w[2], cols[:, R_CONVB + j:R_CONVB + j + 1],
                                     ALU.mult, ALU.add))
                link(V.scalar_tensor_tensor(ct[:, 1, :], v_sb[:, s, 1:T + 1], w[1], ct[:, 0, :], ALU.mult, ALU.add))
                link(V.scalar_tensor_tensor(ct[:, 0, :], v_sb[:, s, 0:T], w[0], ct[:, 1, :], ALU.mult, ALU.add))
                V.tensor_tensor(z_sb[:, j, :], bank[2 * s + 1][:, 0:T], ct[:, 0, :], ALU.mult).then_inc(z_ready, 1)
                dve.wait_ge(z_ready, j + 1)

            def s5_step(t):
                b, q = t // 4, t % 4
                cos, sin = rot[:, b % 2, 0, q, :], rot[:, b % 2, 1, q, :]
                if q == 0:
                    dve.wait_ge(rot_ready, b + 1)
                dve.wait_ge(bu_psum, t + 1)
                bu = bank[4 + t % 2][:].rearrange("p (i t) -> p i t", i=2)
                cos2, sin2 = (w.unsqueeze(1).to_broadcast([P, 2, T]) for w in (cos, sin))
                V.tensor_tensor(turned[:, 0], bu, cos2, ALU.mult)
                V.tensor_tensor(turned[:, 1], bu, sin2, ALU.mult).then_inc(bu_used, 1)
                dve.wait_ge(bu_used, t + 1)
                zin, zst = turned[:, 0], turned[:, 1]
                V.tensor_tensor(zin[:, 0, :], turned[:, 0, 0, :], turned[:, 1, 1, :], ALU.add)
                link(V.tensor_tensor(zin[:, 1, :], turned[:, 0, 1, :], turned[:, 1, 0, :], ALU.subtract))
                rho = s5c[:, 2, t:t + 1].to_broadcast([P, T])
                V.tensor_tensor_scan(zst[:, 0, :], rho, zin[:, 0, :], 0.0, ALU.mult, ALU.add)
                link(V.tensor_tensor_scan(zst[:, 1, :], rho, zin[:, 1, :], 0.0, ALU.mult, ALU.add))
                if t >= 2:
                    dve.wait_ge(q_used, t - 1)
                V.tensor_tensor(q_sb[:, t % 2, 0], zst, cos2, ALU.mult)
                ins = V.tensor_tensor(q_sb[:, t % 2, 1], zst, sin2, ALU.mult)
                ins.then_inc(q_ready, 1)
                dve.wait_ge(q_ready, t + 1)
                if q == 3:
                    V.tensor_copy(par[:, 0:1], par[:, 1:2]).then_inc(rot_used, 1)
                    dve.wait_ge(rot_used, b + 1)

            def y_pre(b):
                dve.wait_ge(q_used, 4 * b + 4)
                V.scalar_tensor_tensor(yT[:, b, :], uT[:, b, :], cols[:, R_SSMD + b:R_SSMD + b + 1],
                                       bank[6 + b % 2][:, 0:T], ALU.mult, ALU.add).then_inc(ypre_ready, 1)

            def main(g):
                if g < 24 and g % 3 == 2:
                    conv(g // 3)
                elif 32 <= g < 40:
                    n = g - 32
                    dve.wait_ge(ga_ready, n + 1)
                    V.tensor_tensor(mixed[:, n, :], mixed[:, n, :], gate[:, n % 2, :], ALU.mult).then_inc(ga_used, 1)

            def s5(t):
                if t < ST:
                    s5_step(t)
                if t >= 6 and (t - 6) % 4 == 0:
                    y_pre((t - 6) // 4)

            for what, n in SCHEDULE:
                main(n) if what == "main" else s5(n)
            y_pre(YB - 1)
            dve.wait_ge(gb_ready, KD)
            dve.wait_ge(ga_used, KD)
            for n in range(KD):
                dve.wait_ge(glu_sig, n + 1)
                dve.wait_ge(glu_psum, 2 * n + 2)
                link(V.tensor_tensor(xs[:, 0, :], bank[2 * (n % 2) + 1][:, 0:T], gate[:, n % 2, :], ALU.mult))
                link(V.tensor_tensor(xs[:, 1, :], xs[:, 0, :], z_sb[:, n, :], ALU.mult))
                V.tensor_tensor(mixed[:, n, :], mixed[:, n, :], xs[:, 1, :], ALU.add).then_inc(mixed_ready, 1)
                dve.wait_ge(mixed_ready, n + 1)
            dve.wait_ge(wo_psum, 1)
            for b in range(TB):
                dve.wait_ge(x_in_s[b], 32)
                for h in range(2):
                    xs_h = x_sb[:, b, 512 * h:512 * h + 512]
                    V.tensor_tensor(xs_h, bank[4 + 2 * b + h][:], xs_h, ALU.add).then_inc(x2_ready, 1)
            dve.wait_ge(sumsq, 4)
            mean_square()
            dve.wait_ge(rstd, 2)
            dve.wait_ge(ffn_in, 16)
            for b in range(TB):
                V.scalar_tensor_tensor(h2[:, b].rearrange("p k q -> p q k"),
                                       x_sb[:, b, :].rearrange("p (q k) -> p q k", k=KD), stat[:, 4 + b:5 + b],
                                       g_ffn.rearrange("p (q k) -> p q k", k=KD), ALU.mult, ALU.mult)\
                    .then_inc(h2_ready, 1)
            for k in ODD_BANKS:
                dve.wait_ge(h2T_psum, k - k % 2 + 2)
                V.tensor_copy(hT[:, k, :], psum_half(8 + k)).then_inc(hT_dve, 1)

            def per_token(ap, n):
                return ap.unsqueeze(2).to_broadcast([P, TB, n])

            def over_tokens(ap, n):
                return ap.unsqueeze(1).to_broadcast([P, TB, n])

            def rcol(i, n=NE):
                return rt[:, :, i, 0:n]

            def first_match(hot, values, best, n, tmp):
                link(V.tensor_tensor(tmp, values, per_token(best, n), ALU.is_equal))
                link(V.scalar_tensor_tensor(tmp, tmp, -64.0, over_tokens(iota[:, 0:n], n), ALU.mult, ALU.add))
                link(V.tensor_reduce(rs[:, 15, :], tmp, AX.X, ALU.min))
                link(V.tensor_tensor(hot, tmp, per_token(rs[:, 15, :], n), ALU.is_equal))

            dve.wait_ge(logits_psum, 1)
            dve.wait_ge(route_in, 64)
            logits = bank[4][:, 0:TB * (NEG + NE)].rearrange("p (b n) -> p b n", b=TB)
            V.tensor_tensor(rcol(2, NEG), logits[:, :, 0:NEG], over_tokens(br[:, 0:NEG], NEG), ALU.add)
            link(V.tensor_tensor(rcol(3), logits[:, :, NEG:], over_tokens(br[:, NEG:], NE), ALU.add))
            link(V.tensor_reduce(rs[:, 0, :], rcol(2, NEG), AX.X, ALU.max))
            V.tensor_tensor(rcol(0, NEG), rcol(2, NEG), per_token(rs[:, 0, :], NEG), ALU.subtract).then_inc(expin_ready, 1)
            first_match(rcol(4, NEG), rcol(2, NEG), rs[:, 0, :], NEG, rcol(5, NEG))
            link(V.tensor_scalar(rcol(5, NEG), rcol(4, NEG), -MASKED, MASKED, ALU.mult, ALU.add))
            for b in range(TB):
                ins = V.tensor_tensor(rt[:, b, 6, :].rearrange("p (g e) -> p g e", g=NEG),
                                      rt[:, b, 3, :].rearrange("p (g e) -> p g e", g=NEG),
                                      rt[:, b, 5, 0:NEG].unsqueeze(2).to_broadcast([P, NEG, EG]), ALU.add)
            link(ins)
            link(V.tensor_reduce(rs[:, 1, :], rcol(6), AX.X, ALU.max))
            first_match(rcol(7), rcol(6), rs[:, 1, :], NE, rcol(9))
            link(V.scalar_tensor_tensor(rcol(6), rcol(7), 3.0 * MASKED, rcol(6), ALU.mult, ALU.add))
            link(V.tensor_reduce(rs[:, 2, :], rcol(6), AX.X, ALU.max))
            V.tensor_tensor(rs[:, 8, :], rs[:, 2, :], rs[:, 1, :], ALU.subtract).then_inc(expin_ready, 1)
            first_match(rcol(8), rcol(6), rs[:, 2, :], NE, rcol(9))
            V.tensor_tensor(member, rcol(7), rcol(8), ALU.add).then_inc(member_ready, 1)
            dve.wait_ge(exp_ready, 2)
            V.tensor_scalar(rs[:, 10, :], rs[:, 9, :], 1.0, None, ALU.add)
            link(V.tensor_reduce(rs[:, 11, :], rcol(1, NEG), AX.X, ALU.add))
            link(V.tensor_tensor(rs[:, 12, :], rs[:, 10, :], rs[:, 11, :], ALU.mult))
            link(V.reciprocal(rs[:, 13, :], rs[:, 12, :]))
            link(V.tensor_tensor(rs[:, 14, :], rs[:, 13, :], rs[:, 9, :], ALU.mult))
            V.tensor_tensor(rcol(9), rcol(7), per_token(rs[:, 13, :], NE), ALU.mult)
            link(V.tensor_tensor(rcol(10), rcol(8), per_token(rs[:, 14, :], NE), ALU.mult))
            V.tensor_tensor(weight, rcol(9), rcol(10), ALU.add)
            link(V.tensor_scalar(rcol(11), member, -UNSELECTED, UNSELECTED, ALU.mult, ALU.add))
            dve.wait_ge(rank_psum, 1)
            link(V.tensor_reduce(cnt_f[:], bank[5][:, 2 * NE:3 * NE], AX.X, ALU.max))
            V.tensor_copy(most[:], cnt_f[:]).then_inc(most_ready, 1)
            link(V.tensor_tensor(rank, rcol(11), bank[5][:, 0:2 * NE].rearrange("p (b n) -> p b n", b=TB), ALU.add))

            dve.wait_ge(most_ready, 1)
            most_r = dve.value_load(most[0:1, 0:1], min_val=0, max_val=T)
            with dve.Fori(0, ROUNDS) as rnd:
                with dve.If(most_r > rnd * SLOTS):
                    with dve.Fori(0, BODIES) as it:
                        for pk in range(BODY_PACKS):
                            done = rnd * PACKS + it * BODY_PACKS + (pk + 1)
                            first = it * (BODY_PACKS * PACK) + pk * PACK
                            shape = [P, TB, PACK, SLOTS]
                            dve.wait_ge(slots_moved, rnd + 1)
                            V.tensor_tensor(sel, slot_no[:].unsqueeze(1).unsqueeze(1).to_broadcast(shape),
                                            rank[:, :, bass.ds(first, PACK)].unsqueeze(3).to_broadcast(shape),
                                            ALU.is_equal).then_inc(sel_ready, 1)
                            dve.wait_ge(sel_ready, done)
                            V.tensor_tensor(wsel, sel,
                                            weight[:, :, bass.ds(first, PACK)].unsqueeze(3).to_broadcast(shape),
                                            ALU.mult).then_inc(wsel_ready, 1)
                            dve.wait_ge(gather_psum, done)
                            V.tensor_copy(xT[:, 4:8, :], bank[7][:].rearrange("p (k s) -> p k s", k=4)).then_inc(xT_dve, 1)
                            dve.wait_ge(silu_ready, done)
                            dve.wait_ge(up_psum, done)
                            V.tensor_tensor(act_sb.rearrange("p c q -> p q c"),
                                            silu.rearrange("p (q c) -> p q c", c=KF),
                                            bank[5][:].rearrange("p (q c) -> p q c", c=KF), ALU.mult).then_inc(act_ready, 1)
                            dve.wait_ge(down_psum, done)
                            V.tensor_copy(y_sb[:, 512:D], bank[7][:]).then_inc(y_dve, 1)
                    V.tensor_scalar(slot_no[:], slot_no[:], float(SLOTS), None, ALU.add).then_inc(slots_moved, 1)
            dve.wait_ge(sumsq, 8)
            link(V.tensor_tensor(stat[:, 0:2], stat[:, 6:10:2], stat[:, 7:11:2], ALU.add))
            mean_square()
            dve.wait_ge(rstd, 3)
            dve.wait_ge(fin_in, 16)
            for b in range(TB):
                for h in range(2):
                    ins = V.scalar_tensor_tensor(x_sb[:, b, 512 * h:512 * h + 512], bank[2 * b + h][:],
                                                 stat[:, 4 + b:5 + b], g_fin[:, 512 * h:512 * h + 512], ALU.mult, ALU.mult)
                ins.then_inc(out_ready, 1)

        @block.tensor
        def _(pe):
            MM = nc.tensor.matmul

            pe.wait_ge(consts, 1)
            pe.wait_ge(rows_in, 16 * 8)
            nc.tensor.transpose(bank[0][:, 0:N_ROWS], rows[:], ident[0:N_ROWS, 0:N_ROWS])
            MM(bank[0][:, 128:128 + GROUPS], ones[0:1, :], logdt_row[:], start=True, stop=True).then_inc(cols_psum, 1)
            xn = mixed[:].rearrange("p k t -> p (k t)").rearrange("p (b d) -> p b d", b=TB)
            for b in range(TB):
                pe.wait_ge(xn_ready, b + 1)
                for k in range(KD):
                    ins = nc.tensor.transpose(psum_half(8 + k)[:, b * P:(b + 1) * P], xn[:, b, k * P:(k + 1) * P], ident[:])
                    if b == TB - 1:
                        ins.then_inc(hT_psum, 1)
            pe.wait_ge(hT_act, KD // 2)
            pe.wait_ge(hT_dve, KD // 2)

            def project(dst, w, n, rhs, done, kn=KD):
                for k in range(kn):
                    ins = MM(dst, w[:, k, n * P:(n + 1) * P], rhs[:, k, :], start=k == 0, stop=k == kn - 1)
                return ins.then_inc(done, 1)

            mix_loaded(pe, U_U)
            for n in range(YB):
                project(psum_half(4 + n), w8(U_U), n, hT, u_psum)
            pe.wait_ge(u_psum, YB)
            pe.wait_ge(zb_ready, 1)
            for i in range(2):
                for b in range(YB):
                    ins = nc.tensor.transpose(bank[4 + i][:, b * P:(b + 1) * P],
                                              zb[:, i, 4 * b:4 * b + 4, :].rearrange("p t h -> p (t h)"), ident[:])
            ins.then_inc(bt_psum, 1)
            pe.wait_ge(zc_ready, 1)
            for i in range(2):
                for b in range(YB):
                    ins = nc.tensor.transpose(bank[6 + i][:, b * P:(b + 1) * P],
                                              zc[:, i, b].rearrange("p g n -> p (g n)"), ident[:])
            ins.then_inc(bt_psum, 1)

            def main(g):
                if g < 24:
                    j, part = g // 3, g % 3
                    unit = U_XBC + 3 * (j // 4) + part
                    if g == 0:
                        pe.wait_ge(cols_ready, 2)
                    if g == 3:
                        pe.wait_ge(u_ready, YB)
                    if part == 0 and j >= 2:
                        pe.wait_ge(z_ready, j - 1)
                    mix_loaded(pe, unit)
                    s = 2 * (j % 2)
                    dst = (bank[s][:, 0:T], bank[s + 1][:, 0:T], bank[s + 1][:, T:2 * T])[part]
                    project(dst, w8(unit), j % 4, hT, xbc_psum)
                elif g < 32:
                    n = g - 24
                    if n == 0:
                        pe.wait_ge(z_ready, KD)
                    if n >= 4:
                        pe.wait_ge(ya_ready, n - 3)
                    mix_loaded(pe, U_CO + n // 4)
                    project(bank[n % 4][:, 0:T], w8(U_CO + n // 4), n % 4, z_sb, ya_psum)
                elif g < 40:
                    n = g - 32
                    pe.wait_ge(*((ya_ready, n + 5) if n < 4 else (ga_ready, n - 3)))
                    mix_loaded(pe, U_GA + n // 4)
                    project(bank[n % 4][:, 0:T], w8(U_GA + n // 4), n % 4, hT, ga_psum)
                else:
                    n = g - 40
                    pe.wait_ge(*((ga_ready, n + 5) if n < 4 else (gb_ready, n - 3)))
                    mix_loaded(pe, U_GB + n // 4)
                    project(bank[n % 4][:, 0:T], w8(U_GB + n // 4), n % 4, hT, gb_psum)
                if g == 0:
                    pe.wait_ge(u_psum, YB)
                    pe.sem_inc(units_used, 1)
                if g in (11, 23):
                    pe.wait_ge(xbc_psum, g + 1)
                    pe.sem_inc(units_used, 3)
                if g >= 24 and g % 4 == 3:
                    pe.wait_ge((ya_psum, ga_psum, gb_psum)[(g - 24) // 8], g % 8 + 1)
                    pe.sem_inc(units_used, 1)

            def s5(t):
                if t < ST and t % 2 == 0:
                    b, q = t // 4, t % 4
                    if t == 0:
                        pe.wait_ge(bt_ready, 1)
                        pe.wait_ge(u_ready, YB)
                    if t >= 2:
                        pe.wait_ge(bu_used, t)
                    for i in range(2):
                        for n in range(2):
                            r = slice(32 * (q + n), 32 * (q + n) + 32)
                            ins = MM(bank[4 + n][:, i * T:(i + 1) * T], BT[r, b, i, :], uT[r, b, :],
                                     start=True, stop=True)
                    ins.then_inc(bu_psum, 2)
                if t >= S5_LAG:
                    t -= S5_LAG
                    b, q = t // 4, t % 4
                    if t == 0:
                        pe.wait_ge(ct_ready, 1)
                    if q == 0 and b >= 2:
                        pe.wait_ge(ypre_ready, b - 1)
                    pe.wait_ge(s_ready, t + 1)
                    c = slice(32 * q, 32 * q + 32)
                    y = bank[6 + b % 2][c, 0:T]
                    for i in range(2):
                        ins = MM(y, CT[:, i, b, c], q_sb[:, t % 2, 0, i, :], start=i == 0, stop=i == 1)
                    ins.then_inc(q_used, 1)

            for what, n in SCHEDULE:
                main(n) if what == "main" else s5(n)

            def project_out(k):
                pe.wait_ge(mixed_ready, k + 1)
                mix_loaded(pe, U_WO + k // 4)
                for b in range(TB):
                    for h in range(2):
                        ins = MM(bank[4 + 2 * b + h][:], mixed[:, k, b * P:(b + 1) * P],
                                 w4(U_WO + k // 4)[:, k % 4, 512 * h:512 * h + 512], start=k == 0, stop=k == KD - 1)
                if k == KD - 1:
                    ins.then_inc(wo_psum, 1)

            pe.wait_ge(y_ready, YB)
            pe.wait_ge(gb_ready, KD)
            for n in range(KD):
                if n >= 2:
                    pe.wait_ge(mixed_ready, n - 1)
                for i, unit in enumerate((U_GLUB, U_GLUA)):
                    mix_loaded(pe, unit)
                    project(bank[2 * (n % 2) + i][:, 0:T], w4(unit), n, yT, glu_psum, YB)
                if n == KD - 1:
                    pe.wait_ge(glu_psum, 2 * KD)
                    pe.sem_inc(units_used, 3)
                if n >= 1:
                    project_out(n - 1)
            project_out(KD - 1)
            pe.wait_ge(wo_psum, 1)
            pe.sem_inc(units_used, 1)

            for b in range(TB):
                for h in range(2):
                    pe.wait_ge(x2_ready, 2 * b + h + 1)
                    MM(bank[2 * b + h][:], ident[:], x_sb[:, b, 512 * h:512 * h + 512], start=True, stop=False)
            for b in range(TB):
                pe.wait_ge(h2_ready, b + 1)
                for k in range(KD):
                    ins = nc.tensor.transpose(psum_half(8 + k)[:, b * P:(b + 1) * P], h2[:, b, k, :], ident[:])
                    if b == TB - 1:
                        ins.then_inc(h2T_psum, 1)
            pe.wait_ge(hT_act, KD)
            pe.wait_ge(hT_dve, KD)
            pe.wait_ge(route_in, 64)
            for b in range(TB):
                n = NEG + NE
                for k in range(KD):
                    ins = MM(bank[4][:, b * n:(b + 1) * n], hT[:, k, b * P:(b + 1) * P], wr[:, k, :],
                             start=k == 0, stop=k == KD - 1)
            ins.then_inc(logits_psum, 1)
            pe.wait_ge(member_ready, 1)
            MM(bank[5][:, 0:NE], upper[:], member[:, 0, :], start=True, stop=True)
            MM(bank[5][:, NE:2 * NE], ones[:], member[:, 0, :], start=True, stop=False)
            MM(bank[5][:, NE:2 * NE], upper[:], member[:, 1, :], start=False, stop=True)
            MM(bank[5][:, 2 * NE:3 * NE], ones[:], member[:, 0, :], start=True, stop=False)
            MM(bank[5][:, 2 * NE:3 * NE], ones[:], member[:, 1, :], start=False, stop=True).then_inc(rank_psum, 1)

            pe.wait_ge(most_ready, 1)
            most_r = pe.value_load(most[0:1, 0:1], min_val=0, max_val=T)
            with pe.Fori(0, ROUNDS) as rnd:
                with pe.If(most_r > rnd * SLOTS):
                    with pe.Fori(0, BODIES) as it:
                        for pk in range(BODY_PACKS):
                            done = rnd * PACKS + it * BODY_PACKS + (pk + 1)

                            def unit(w):
                                u = MIX_UNITS + pk * PACK_UNITS + w
                                fills = rnd * (ROUND_UNITS // RING) + it * (BODY_UNITS // RING) + (u // RING + 1)
                                pe.wait_ge(loaded[u % RING], fills * 16)
                                return ring[:, u % RING, :].rearrange("p (e n) -> p e n", e=PACK)

                            pe.wait_ge(sel_ready, done)
                            for k in range(KD):
                                for b in range(TB):
                                    ins = MM(bank[6 + k // 4][:, (k % 4) * P:(k % 4 + 1) * P], h2[:, b, k, :],
                                             sel[:, b].rearrange("p e s -> p (e s)"), start=b == 0, stop=b == TB - 1)
                            ins.then_inc(gather_psum, 1)
                            pe.wait_ge(wsel_ready, done)
                            for b in range(TB):
                                ins = nc.tensor.transpose(bank[5][:, b * P:(b + 1) * P],
                                                          wsel[:, b].rearrange("p e s -> p (e s)"), ident[:])
                            ins.then_inc(wselT_psum, 1)
                            pe.wait_ge(xT_act, done)
                            pe.wait_ge(xT_dve, done)
                            pe.wait_ge(wselT_ready, done)
                            for w in range(8):
                                wt = unit(w)
                                for kk in range(2):
                                    k = 2 * (w // 2) + kk
                                    for e in range(PACK):
                                        q = slice(SLOTS * e, SLOTS * e + SLOTS)
                                        ins = MM(bank[4 + w % 2][q, :], xT[:, k, q], wt[:, e, 512 * kk:512 * kk + 512],
                                                 start=k == 0, stop=k == KD - 1)
                                if w < 7:
                                    ins.then_inc(units_used, 1)
                                else:
                                    ins.then_inc(up_psum, 1)
                            pe.wait_ge(up_psum, done)
                            pe.sem_inc(units_used, 1)
                            pe.wait_ge(act_ready, done)
                            for c in range(KF):
                                ins = nc.tensor.transpose(bank[4][:, c * P:(c + 1) * P], act_sb[:, c, :], ident[:])
                            ins.then_inc(actT_psum, 1)
                            pe.wait_ge(actT_ready, done)
                            for c in range(KF):
                                wt = unit(8 + c)
                                for e in range(PACK):
                                    q = slice(SLOTS * e, SLOTS * e + SLOTS)
                                    for h in range(2):
                                        ins = MM(bank[6 + h][q, :], actT[:, c, q], wt[:, e, 512 * h:512 * h + 512],
                                                 start=c == 0, stop=c == KF - 1)
                                if c < KF - 1:
                                    ins.then_inc(units_used, 1)
                                else:
                                    ins.then_inc(down_psum, 1)
                            pe.wait_ge(down_psum, done)
                            pe.sem_inc(units_used, 1)
                            pe.wait_ge(y_act, done)
                            pe.wait_ge(y_dve, done)
                            for b in range(TB):
                                for h in range(2):
                                    MM(bank[2 * b + h][:], wselT[:, b, :], y_sb[:, 512 * h:512 * h + 512],
                                       start=False, stop=False)
            for i in range(4):
                ins = MM(bank[i][:], zeros[:, 0:P], zeros[:], start=False, stop=True)
            ins.then_inc(moe_psum, 1)


_INS = ["x", "norm_mix", "w_in", "conv_w", "conv_b", "w_conv_out", "ssm_a_re", "ssm_a_im", "ssm_log_dt",
        "ssm_b_re", "ssm_b_im", "ssm_c_re", "ssm_c_im", "ssm_d", "w_glu_a", "w_glu_b", "gate_bias", "w_o",
        "norm_ffn", "w_route_group", "b_route_group", "w_route_expert", "b_route_expert", "w_gate", "w_up",
        "w_down", "norm_final"]


def kernel(**inputs):
    import numpy as np
    import concourse.bacc as bacc
    from concourse.bass_utils import run_bass_kernel_spmd

    nc = bacc.Bacc("TRN2", target_bir_lowering=False, num_devices=1, dynamic_dma_scratch_size=1024)
    arrays, args = {}, []
    for name in _INS:
        a = np.ascontiguousarray(inputs[name])
        arrays[f"in_{name}"] = a
        args.append(nc.dram_tensor(f"in_{name}", a.shape, mybir.dt.from_np(a.dtype), kind="ExternalInput").ap())
    args.append(nc.dram_tensor("out_dram", (1, T, D), mybir.dt.float32, kind="ExternalOutput").ap())
    block_kernel(nc, *args)
    r = run_bass_kernel_spmd(nc, [arrays], core_ids=[0])
    return r.results[0]["out_dram"]
```

```python
from contextlib import ExitStack

import concourse.bass as bass
from concourse import mybir

D = 1024
T = 256
P = 128
KD = D // P
TB = T // P
SSM = 512
YB = SSM // P
GROUPS, STATE, GH = 32, 64, 16
ST = GROUPS * STATE // P
NEG, EG, NE = 4, 8, 32
FF = 512
KF = FF // P
EPS = 1e-6

UNIT = 4096
RING = 8
MIX_UNITS = 17
SLOTS = 32
PACK = P // SLOTS
PACKS = NE // PACK
PACK_UNITS = 12
ROUND_UNITS = PACKS * PACK_UNITS
BODY_PACKS = 2
BODY_UNITS = BODY_PACKS * PACK_UNITS
BODIES = PACKS // BODY_PACKS
ROUNDS = T // SLOTS
UNSELECTED = 1.0e4

TWO_PI = 6.283185307179586
PI_HI, PI_MID = 6.28125, 0.0019350051879882812
PI_LO = TWO_PI - PI_HI - PI_MID
ROUNDER = 12582912.0
PI_CLAMP = 3.1415925
EULER = 2.718281828459045
MASKED = -1.0e30

R_GMIX, R_CONVW, R_CONVB, R_GATEB, R_SSMD, R_ARE, R_AIM, N_ROWS = 0, 8, 32, 40, 56, 60, 76, 92

EVEN_BANKS, ODD_BANKS = (0, 1, 4, 5), (2, 3, 6, 7)

N_MAIN = 48
S5_LAG = 2


def mixer_schedule():
    order, step = [], 0
    for g in range(N_MAIN):
        order.append(("main", g))
        if g >= 4 and g % 2 == 0 and step < ST + S5_LAG:
            order.append(("s5", step))
            step += 1
    while step < ST + S5_LAG:
        order.append(("s5", step))
        step += 1
    return order


def block_kernel(nc, x_in, norm_mix, w_in, conv_w, conv_b, w_conv_out, a_re, a_im, log_dt, b_re, b_im,
                 c_re, c_im, ssm_d, w_glu_a, w_glu_b, gate_bias, w_o, norm_ffn, w_rg, b_rg, w_re, b_re_,
                 w_gate, w_up, w_down, norm_final, out):
    f32 = mybir.dt.float32
    i32 = mybir.dt.int32
    bf16 = mybir.dt.bfloat16
    ALU = mybir.AluOpType
    ACT = mybir.ActivationFunctionType
    AX = mybir.AxisListType
    SCHEDULE = mixer_schedule()

    ctx = ExitStack()
    with ctx:
        def sb(name, shape, dt=f32):
            return ctx.enter_context(nc.sbuf_tensor(name, shape, dt))

        def sem(name):
            return ctx.enter_context(nc.semaphore(name))

        ring = sb("ring", [P, RING, UNIT])
        hT = sb("hT", [P, KD, T])
        rows = sb("rows", [N_ROWS, P])
        cols = sb("cols", [P, 128])
        logdt_row = sb("logdt_row", [1, GROUPS])
        ident = sb("ident", [P, P])
        ones = sb("ones", [P, P])
        s5c = sb("s5c", [P, 16, ST])
        dt_t = sb("dt_t", [P, ST])
        eul = sb("eul", [P, ST])
        par_i = sb("par_i", [P, 1], i32)
        par = sb("par", [P, 2])
        ptmp = sb("ptmp", [P, 2, ST, 8])
        stat = sb("stat", [P, 12])
        halfneg = sb("halfneg", [P, 2])
        wr = sb("wr", [P, KD, NEG + NE])
        br = sb("br", [P, NEG + NE])
        rs = sb("rs", [P, 16, TB])
        iota = sb("iota", [P, NE])
        slot_no = sb("slot_no", [P, SLOTS])
        member = sb("member", [P, TB, NE], bf16)
        upper16 = sb("upper16", [P, P], bf16)
        ones16 = sb("ones16", [P, P], bf16)
        cnt_f = sb("cnt_f", [P, 1])
        most = sb("most", [P, 1], i32)

        def region(name, n):
            flat = sb(name, [P, n])

            def view(at, *shape):
                size = 1
                for d in shape:
                    size *= d
                assert at + size <= n
                names = "abcd"[:len(shape)]
                form = f"p ({' '.join(names)}) -> p {' '.join(names)}"
                return flat[:, at:at + size].rearrange(form, **dict(zip(names, shape)))
            return view

        x_region = region("x_region", TB * D)
        x_sb = x_region(0, TB, D)
        rtmp = x_region(0, 4, T)
        turned = x_region(4 * T, 2, 2, T)
        h2_region = region("h2_region", TB * D)
        zb = h2_region(0, 2, ST, 2 * GH)
        zc = h2_region(D, 2, YB, 2, STATE)
        s_sb = h2_region(0, 4, 2, T)
        h2 = h2_region(0, TB, KD, P)
        m_region = region("m_region", KD * T)
        xn = m_region(0, TB, D)
        mixed = m_region(0, KD, T)
        y_sb = m_region(0, D)
        actT = m_region(D, KF, P)
        z_region = region("z_region", KD * T)
        bld = z_region(0, 2, ST, GH)
        btmp = z_region(512, 4, ST, GH)
        cld = z_region(1536, 2, YB, STATE)
        z_sb = z_region(0, KD, T)
        xT = z_region(0, KD, P)
        silu = z_region(1024, FF)
        act_sb = z_region(1536, KF, P)
        u_region = region("u_region", D)
        uT = u_region(0, YB, T)
        g_ffn = u_region(0, D)
        y_region = region("y_region", D)
        yT = y_region(0, YB, T)
        g_fin = y_region(0, D)
        conv_region = region("conv_region", 8 * T + 8)
        xs = conv_region(0, 2, T)
        v_sb = conv_region(2 * T, 2, T + 2)
        ct = conv_region(4 * T + 4, 2, T)
        gate = conv_region(6 * T + 4, 2, T)
        rt = conv_region(0, TB, 12, NE)
        sel = conv_region(768, TB, PACK, SLOTS)
        wsel = conv_region(1024, TB, PACK, SLOTS)
        wselT = conv_region(1280, TB, P)
        weight = conv_region(1536, TB, NE)
        rank = conv_region(1600, TB, NE)
        s5_region = region("s5_region", UNIT)
        BT = s5_region(0, YB, 2, P)
        CT = s5_region(1024, 2, YB, P)
        sprod = s5_region(2048, 2, 2, T)
        lowT = s5_region(3072, 2, ST, 16)
        highT = s5_region(3584, 2, ST, 16)
        extra1 = s5_region(0, UNIT)
        rot_region = region("rot_region", UNIT)
        rot = rot_region(0, 2, 2, 4, T)
        extra0 = rot_region(0, UNIT)

        bank = [ctx.enter_context(nc.psum_tensor(f"bank{i}", [P, 512], f32)) for i in range(8)]

        loaded = [sem(f"loaded{i}") for i in range(RING)]
        extra_in = [sem(f"extra_in{i}") for i in range(2)]
        units_used = sem("units_used")
        x_in_s = [sem(f"x_in{i}") for i in range(TB)]
        rows_in = sem("rows_in")
        b_in = sem("b_in")
        c_in = sem("c_in")
        route_in = sem("route_in")
        ffn_in = sem("ffn_in")
        fin_in = sem("fin_in")
        consts = sem("consts")
        pool_step = sem("pool_step")
        act_step = sem("act_step")
        dve_step = sem("dve_step")
        sumsq = sem("sumsq")
        meansq = sem("meansq")
        rstd = sem("rstd")
        xn_ready = sem("xn_ready")
        cols_psum = sem("cols_psum")
        cols_ready = sem("cols_ready")
        dt_ready = sem("dt_ready")
        hT_psum = sem("hT_psum")
        hT_act = sem("hT_act")
        hT_dve = sem("hT_dve")
        u_psum = sem("u_psum")
        u_ready = sem("u_ready")
        expo_ready = sem("expo_ready")
        rho_ready = sem("rho_ready")
        angle_ready = sem("angle_ready")
        sines_ready = sem("sines_ready")
        zb_ready = sem("zb_ready")
        zc_ready = sem("zc_ready")
        bt_psum = sem("bt_psum")
        bt_ready = sem("bt_ready")
        ct_ready = sem("ct_ready")
        powers_ready = sem("powers_ready")
        rot_ready = sem("rot_ready")
        rot_used = sem("rot_used")
        bu_psum = sem("bu_psum")
        bu_used = sem("bu_used")
        q_ready = sem("q_ready")
        s_ready = sem("s_ready")
        q_used = sem("q_used")
        ypre_ready = sem("ypre_ready")
        y_ready = sem("y_ready")
        xbc_psum = sem("xbc_psum")
        xs_ready = sem("xs_ready")
        z_ready = sem("z_ready")
        ya_psum = sem("ya_psum")
        ya_ready = sem("ya_ready")
        ga_psum = sem("ga_psum")
        ga_ready = sem("ga_ready")
        ga_used = sem("ga_used")
        gb_psum = sem("gb_psum")
        gb_ready = sem("gb_ready")
        glu_psum = sem("glu_psum")
        glu_sig = sem("glu_sig")
        mixed_ready = sem("mixed_ready")
        wo_psum = sem("wo_psum")
        x2_ready = sem("x2_ready")
        xg_dve = sem("xg_dve")
        xg_pool = sem("xg_pool")
        h2_ready = sem("h2_ready")
        h2T_psum = sem("h2T_psum")
        logits_psum = sem("logits_psum")
        expin_ready = sem("expin_ready")
        exp_ready = sem("exp_ready")
        member_ready = sem("member_ready")
        rank_psum = sem("rank_psum")
        most_ready = sem("most_ready")
        sel_ready = sem("sel_ready")
        wsel_ready = sem("wsel_ready")
        gather_psum = sem("gather_psum")
        wselT_psum = sem("wselT_psum")
        wselT_ready = sem("wselT_ready")
        xT_act = sem("xT_act")
        xT_dve = sem("xT_dve")
        up_psum = sem("up_psum")
        silu_ready = sem("silu_ready")
        act_ready = sem("act_ready")
        actT_psum = sem("actT_psum")
        actT_ready = sem("actT_ready")
        down_psum = sem("down_psum")
        y_act = sem("y_act")
        y_dve = sem("y_dve")
        slots_moved = sem("slots_moved")
        moe_psum = sem("moe_psum")
        fg_ready = sem("fg_ready")
        out_act = sem("out_act")
        out_dve = sem("out_dve")
        stored = sem("stored")

        extra = (extra0, extra1)
        SKIPPED = [(MIX_UNITS + v) % RING for v in range(len(extra))]

        def mix_slot(u):
            return ring[:, u % RING, :]

        def mix_loaded(eng, u):
            eng.wait_ge(loaded[u % RING], 16 * (u // RING + 1))

        def w8(u):
            return mix_slot(u).rearrange("p (k n) -> p k n", k=KD)

        def w4(u):
            return mix_slot(u).rearrange("p (k n) -> p k n", k=4)

        U_U, U_XBC, U_CO, U_GA, U_GB, U_GLUB, U_GLUA, U_WO = 0, 1, 7, 9, 11, 13, 14, 15

        def psum_half(i):
            return bank[i // 2][:, (i % 2) * T:(i % 2) * T + T]

        def scaled_half(b, h):
            half = slice(512 * h, 512 * h + 512)
            return (h2[:, b, :, 64 * h:64 * h + 64].rearrange("p k q -> p q k"),
                    x_sb[:, b, half].rearrange("p (q k) -> p q k", k=KD),
                    g_ffn[:, half].rearrange("p (q k) -> p q k", k=KD))

        block = ctx.enter_context(nc.Block())

        @block.sync
        def _(sp):
            def in_cols(c0):
                return w_in[0].rearrange("(k p) n -> p k n", p=P)[:, :, c0:c0 + 512]

            xbc = [in_cols(part * D + half * 512) for half in range(2) for part in range(3)]
            co = w_conv_out[0].rearrange("(k p) n -> p k n", p=P)
            wo = w_o[0].rearrange("(k p) n -> p k n", p=P)
            sources = [in_cols(3 * D)] + xbc + [co[:, :, 0:512], co[:, :, 512:D]]
            sources += [in_cols(3 * D + SSM + i * 512) for i in range(4)]
            sources += [w_glu_b[0].rearrange("(k p) n -> p k n", p=P), w_glu_a[0].rearrange("(k p) n -> p k n", p=P)]
            sources += [wo[:, 0:4, :], wo[:, 4:8, :]]
            assert len(sources) == MIX_UNITS
            for r, n, src in ((R_GMIX, KD, norm_mix[0]), (R_CONVW, 3 * KD, conv_w[0].rearrange("a b c -> (a b c)")),
                              (R_CONVB, KD, conv_b[0]), (R_GATEB, 2 * KD, gate_bias[0].rearrange("a c -> (a c)")),
                              (R_SSMD, YB, ssm_d[0]), (R_ARE, ST, a_re[0].rearrange("g n -> (g n)")),
                              (R_AIM, ST, a_im[0].rearrange("g n -> (g n)"))):
                sp.dma_start(rows[r:r + n, :], src.rearrange("(r c) -> r c", c=P)).then_inc(rows_in, 16)
            sp.dma_start(logdt_row[:], log_dt[0:1, :]).then_inc(rows_in, 16)
            for u, src in enumerate(sources):
                if u == 1:
                    for i, part in enumerate((b_re, b_im)):
                        sp.dma_start(bld[:, i], part[0].rearrange("(t g) n h -> (g n) t h", g=2)).then_inc(b_in, 16)
                    for i, part in enumerate((c_re, c_im)):
                        sp.dma_start(cld[:, i], part[0].rearrange("(b g) h n -> (g h) b n", g=8)).then_inc(c_in, 16)
                if u == 5:
                    sp.dma_start(wr[:, :, 0:NEG], w_rg[0].rearrange("(p k) n -> p k n", p=P)).then_inc(route_in, 16)
                    sp.dma_start(wr[:, :, NEG:], w_re[0].rearrange("(p k) n -> p k n", p=P)).then_inc(route_in, 16)
                    sp.dma_start(br[:, 0:NEG], b_rg.to_broadcast([P, NEG])).then_inc(route_in, 16)
                    sp.dma_start(br[:, NEG:], b_re_.to_broadcast([P, NE])).then_inc(route_in, 16)
                if u >= RING:
                    sp.wait_ge(units_used, u - RING + 1)
                sp.dma_start(mix_slot(u).rearrange("p (k n) -> p k n", k=src.shape[1]), src).then_inc(loaded[u % RING], 16)

            gate_v = w_gate[0].rearrange("e (p k) n -> p e (k n)", p=P)
            up_v = w_up[0].rearrange("e (p k) n -> p e (k n)", p=P)
            down_v = w_down[0].rearrange("e (p c) n -> p e (c n)", p=P)

            def load_round(used_base):
                with sp.Fori(0, BODIES) as it:
                    for v in range(BODY_UNITS):
                        pk, w = v // PACK_UNITS, v % PACK_UNITS
                        slot = (MIX_UNITS + v) % RING
                        dst, landed = (extra[v], extra_in[v]) if v < len(extra) else (ring[:, slot, :], loaded[slot])
                        first = it * (BODY_PACKS * PACK) + pk * PACK
                        if v >= len(extra):
                            back = 2 * RING if RING <= v < RING + len(extra) else RING
                            sp.wait_ge(units_used, used_base + it * BODY_UNITS + (v + MIX_UNITS - back + 1))
                        if w < 8:
                            view = gate_v if w % 2 == 0 else up_v
                            src = view[:, bass.ds(first, PACK), (w // 2) * 1024:(w // 2 + 1) * 1024]
                        else:
                            src = down_v[:, bass.ds(first, PACK), (w - 8) * D:(w - 7) * D]
                        sp.dma_start(dst.rearrange("p (e n) -> p e n", e=PACK), src).then_inc(landed, 16)

            sp.wait_ge(s_ready, ST)
            sp.wait_ge(q_used, ST)
            load_round(0)
            sp.wait_ge(most_ready, 1)
            most_r = sp.value_load(most[0:1, 0:1], min_val=0, max_val=T)
            with sp.Fori(1, ROUNDS) as rnd:
                with sp.If(most_r > rnd * SLOTS):
                    load_round(rnd * ROUND_UNITS)
            for b, done in ((1, out_dve), (0, out_act)):
                sp.wait_ge(done, 1)
                sp.dma_start(out[0, b * P:(b + 1) * P, :], x_sb[:, b, :]).then_inc(stored, 16)
            sp.wait_ge(stored, 16 * TB)

        @block.gpsimd
        def _(pool):
            steps = [0]

            def link(ins):
                steps[0] += 1
                ins.then_inc(pool_step, 1)
                pool.wait_ge(pool_step, steps[0])

            nc.gpsimd.memset(halfneg[:], -0.5)
            nc.gpsimd.memset(eul[:], EULER)
            nc.gpsimd.memset(ones[:], 1.0)
            nc.gpsimd.memset(ones16[:], 1.0)
            nc.gpsimd.memset(zb, 0.0)
            nc.gpsimd.memset(v_sb, 0.0)
            nc.gpsimd.memset(lowT[:, 1], 0.0)
            nc.gpsimd.memset(highT[:, 1], 0.0)
            nc.gpsimd.memset(lowT[:, 0], 1.0)
            nc.gpsimd.memset(highT[:, 0], 1.0)
            link(nc.gpsimd.memset(ident[:], 0.0))
            nc.gpsimd.affine_select(out=ident[:], in_=ident[:], compare_op=ALU.not_equal, fill=1.0, base=0,
                                    pattern=[[-1, P]], channel_multiplier=1).then_inc(consts, 1)
            nc.gpsimd.affine_select(out=upper16[:], in_=ones[:], compare_op=ALU.is_gt, fill=0.0, base=0,
                                    pattern=[[1, P]], channel_multiplier=-1)
            nc.gpsimd.iota(iota[:], pattern=[[1, NE]], base=0, channel_multiplier=0,
                           allow_small_or_imprecise_dtypes=True)
            nc.gpsimd.iota(slot_no[:], pattern=[[1, SLOTS]], base=0, channel_multiplier=0,
                           allow_small_or_imprecise_dtypes=True).then_inc(slots_moved, 1)
            nc.gpsimd.iota(par_i[:], pattern=[[0, 1]], base=0, channel_multiplier=1).then_inc(consts, 1)
            pool.wait_ge(meansq, 1)
            nc.gpsimd.tensor_tensor(stat[:, 4:6], stat[:, 2:4], halfneg[:], ALU.pow).then_inc(rstd, 1)
            pool.wait_ge(cols_ready, 2)
            nc.gpsimd.tensor_tensor(dt_t[:], eul[:], s5c[:, 0, :], ALU.pow).then_inc(dt_ready, 1)
            pool.wait_ge(expo_ready, 1)
            nc.gpsimd.tensor_tensor(s5c[:, 2, :], eul[:], s5c[:, 1, :], ALU.pow).then_inc(rho_ready, 1)
            pool.wait_ge(powers_ready, 1)

            def rotations(b):
                if b >= 2:
                    pool.wait_ge(rot_used, b - 1)
                lo = [lowT[:, i, 4 * b:4 * b + 4, :].unsqueeze(2).to_broadcast([P, 4, 16, 16]) for i in range(2)]
                hi = [highT[:, i, 4 * b:4 * b + 4, :].unsqueeze(3).to_broadcast([P, 4, 16, 16]) for i in range(2)]
                o = [rot[:, b % 2, i].rearrange("p t (h l) -> p t h l", l=16) for i in range(2)]
                tmp = rtmp.rearrange("p t (h l) -> p t h l", l=16)
                nc.gpsimd.tensor_tensor(o[0], lo[0], hi[0], ALU.mult)
                link(nc.gpsimd.tensor_tensor(tmp, lo[1], hi[1], ALU.mult))
                link(nc.gpsimd.tensor_tensor(o[0], o[0], tmp, ALU.subtract))
                nc.gpsimd.tensor_tensor(o[1], lo[0], hi[1], ALU.mult)
                link(nc.gpsimd.tensor_tensor(tmp, lo[1], hi[0], ALU.mult))
                nc.gpsimd.tensor_tensor(o[1], o[1], tmp, ALU.add).then_inc(rot_ready, 1)
                pool.wait_ge(rot_ready, b + 1)

            def state_sums(t):
                s, sp = s_sb[:, t % 4], sprod[:, t % 2]
                pool.wait_ge(q_ready, t + 1)
                nc.gpsimd.tensor_tensor(s[:, 0, :], s[:, 0, :], sp[:, 1, :], ALU.subtract)
                nc.gpsimd.tensor_tensor(s[:, 1, :], s[:, 1, :], sp[:, 0, :], ALU.add).then_inc(s_ready, 1)

            rotations(0)
            rotations(1)
            for t in range(ST):
                state_sums(t)
                if t % 4 == 3 and t // 4 + 2 < YB:
                    rotations(t // 4 + 2)
            pool.wait_ge(ffn_in, 16)
            for b in range(TB):
                pool.wait_ge(x2_ready, 2 * b + 1)
                nc.gpsimd.tensor_tensor(*scaled_half(b, 0), ALU.mult).then_inc(xg_pool, 1)
            for n in range(2):
                pool.wait_ge(meansq, 2 + n)
                nc.gpsimd.tensor_tensor(stat[:, 4:6], stat[:, 2:4], halfneg[:], ALU.pow).then_inc(rstd, 1)

        @block.scalar
        def _(act):
            steps = [0]

            def link(ins):
                steps[0] += 1
                ins.then_inc(act_step, 1)
                act.wait_ge(act_step, steps[0])

            for b in range(TB):
                act.dma_start(x_sb[:, b, :], x_in[0, b * P:(b + 1) * P, :]).then_inc(x_in_s[b], 16)

            for b in range(TB):
                act.wait_ge(x_in_s[b], 16)
                if b:
                    act.wait_ge(sumsq, b)
                nc.scalar.activation(hT[:, 0:4, :].rearrange("p k t -> p (k t)"), x_sb[:, b, :], ACT.Square, accum_out=stat[:, b:b + 1]).then_inc(sumsq, 1)
            act.wait_ge(cols_psum, 1)
            nc.scalar.activation(cols[:, 0:N_ROWS], bank[0][:, 0:N_ROWS], ACT.Copy).then_inc(cols_ready, 1)
            for g in range(2):
                ins = nc.scalar.activation(s5c[64 * g:64 * g + 64, 0, :],
                                           bank[0][64 * g:64 * g + 64, 128 + g:128 + GROUPS:2], ACT.Copy)
            ins.then_inc(cols_ready, 1)
            act.wait_ge(cols_ready, 2)
            for k in EVEN_BANKS:
                act.wait_ge(hT_psum, k - k % 2 + 2)
                nc.scalar.activation(hT[:, k, :], psum_half(8 + k), ACT.Copy,
                                     scale=cols[:, R_GMIX + k:R_GMIX + k + 1]).then_inc(hT_act, 1)
            act.wait_ge(angle_ready, 1)
            nc.scalar.activation(s5c[:, 5, :], s5c[:, 4, :], ACT.Sin)
            nc.scalar.activation(s5c[:, 6, :], s5c[:, 4, :], ACT.Sin, scale=0.5).then_inc(sines_ready, 1)
            for n in range(YB):
                act.wait_ge(u_psum, n - n % 2 + 2)
                nc.scalar.activation(uT[:, n, :], psum_half(4 + n), ACT.Copy).then_inc(u_ready, 1)
            act.wait_ge(bt_psum, 1)
            for i in range(2):
                ins = nc.scalar.activation(BT[:, :, i, :], bank[4 + i][:].rearrange("p (b n) -> p b n", b=YB), ACT.Copy)
            ins.then_inc(bt_ready, 1)

            def main(g):
                if g < 24:
                    j = g // 3
                    if g % 3 == 0:
                        act.wait_ge(xbc_psum, g + 1)
                        if j >= 2:
                            act.wait_ge(z_ready, j - 1)
                        nc.scalar.activation(xs[:, j % 2, :], bank[2 * (j % 2)][:, 0:T], ACT.Copy).then_inc(xs_ready, 1)
                elif g < 32:
                    n = g - 24
                    act.wait_ge(ya_psum, n + 1)
                    nc.scalar.activation(mixed[:, n, :], bank[n % 4][:, 0:T], ACT.Copy).then_inc(ya_ready, 1)
                elif g < 40:
                    n = g - 32
                    act.wait_ge(ga_psum, n + 1)
                    if n >= 2:
                        act.wait_ge(ga_used, n - 1)
                    nc.scalar.activation(gate[:, n % 2, :], bank[n % 4][:, 0:T], ACT.Sigmoid,
                                         bias=cols[:, R_GATEB + n:R_GATEB + n + 1]).then_inc(ga_ready, 1)
                else:
                    n = g - 40
                    act.wait_ge(gb_psum, n + 1)
                    nc.scalar.activation(z_sb[:, n, :], bank[n % 4][:, 0:T], ACT.Sigmoid,
                                         bias=cols[:, R_GATEB + KD + n:R_GATEB + KD + n + 1]).then_inc(gb_ready, 1)

            def s5(t):
                if t >= 6 and (t - 6) % 4 == 0:
                    gelu((t - 6) // 4)
                if t == ST + S5_LAG - 1:
                    gelu(YB - 1)

            def gelu(b):
                act.wait_ge(ypre_ready, b + 1)
                nc.scalar.activation(yT[:, b, :], yT[:, b, :], ACT.Gelu_apprx_tanh).then_inc(y_ready, 1)

            for what, n in SCHEDULE:
                main(n) if what == "main" else s5(n)
            act.wait_ge(s_ready, ST)
            act.wait_ge(rot_ready, YB)
            for b in range(TB):
                act.dma_start(x_sb[:, b, :], x_in[0, b * P:(b + 1) * P, :]).then_inc(x_in_s[b], 16)
            act.dma_start(g_ffn, norm_ffn.to_broadcast([P, D])).then_inc(ffn_in, 16)
            act.wait_ge(ga_used, KD)
            for n in range(KD):
                act.wait_ge(glu_psum, 2 * n + 1)
                if n >= 2:
                    act.wait_ge(mixed_ready, n - 1)
                nc.scalar.activation(gate[:, n % 2, :], bank[2 * (n % 2)][:, 0:T], ACT.Sigmoid).then_inc(glu_sig, 1)
            act.wait_ge(glu_psum, 2 * KD)
            act.dma_start(g_fin, norm_final.unsqueeze(0).to_broadcast([P, D])).then_inc(fin_in, 16)
            for b in range(TB):
                act.wait_ge(x2_ready, 2 * (b + 1))
                act.wait_ge(sumsq, 2 + b)
                nc.scalar.activation(y_sb, x_sb[:, b, :], ACT.Square, accum_out=stat[:, b:b + 1]).then_inc(sumsq, 1)
            for k in EVEN_BANKS:
                act.wait_ge(h2T_psum, k - k % 2 + 2)
                nc.scalar.activation(hT[:, k, :], psum_half(8 + k), ACT.Copy).then_inc(hT_act, 1)
            act.wait_ge(h2T_psum, KD)
            act.wait_ge(rstd, 2)
            for b in range(TB):
                nc.scalar.activation(h2[:, b], h2[:, b], ACT.Copy, scale=stat[:, 4 + b:5 + b]).then_inc(h2_ready, 1)
            for n in range(2):
                act.wait_ge(expin_ready, n + 1)
                if n == 0:
                    ins = nc.scalar.activation(rt[:, :, 1, 0:NEG], rt[:, :, 0, 0:NEG], ACT.Exp)
                else:
                    ins = nc.scalar.activation(rs[:, 9, :], rs[:, 8, :], ACT.Exp)
                ins.then_inc(exp_ready, 1)

            def experts(rnd):
                with act.Fori(0, BODIES) as it:
                    for pk in range(BODY_PACKS):
                        done = rnd * PACKS + it * BODY_PACKS + (pk + 1)
                        act.wait_ge(gather_psum, done * 2 - 1)
                        nc.scalar.activation(xT[:, 0:4, :], bank[6][:].rearrange("p (k s) -> p k s", k=4),
                                             ACT.Copy).then_inc(xT_act, 1)
                        act.wait_ge(wselT_psum, done)
                        nc.scalar.activation(wselT, bank[5][:, 0:TB * P].rearrange("p (b t) -> p b t", b=TB),
                                             ACT.Copy).then_inc(wselT_ready, 1)
                        act.wait_ge(up_psum, done)
                        nc.scalar.activation(silu, bank[4][:], ACT.Silu).then_inc(silu_ready, 1)
                        act.wait_ge(actT_psum, done)
                        nc.scalar.activation(actT, bank[4][:].rearrange("p (c s) -> p c s", c=KF),
                                             ACT.Copy).then_inc(actT_ready, 1)
                        act.wait_ge(down_psum, done)
                        nc.scalar.activation(y_sb[:, 0:512], bank[6][:], ACT.Copy).then_inc(y_act, 1)

            experts(0)
            act.wait_ge(most_ready, 1)
            most_r = act.value_load(most[0:1, 0:1], min_val=0, max_val=T)
            with act.Fori(1, ROUNDS) as rnd:
                with act.If(most_r > rnd * SLOTS):
                    experts(rnd)
            act.wait_ge(moe_psum, 1)
            for b in range(TB):
                for h in range(2):
                    i = 2 * b + h
                    if b == 1:
                        act.wait_ge(fg_ready, h + 1)
                    nc.scalar.activation(h2[:, b, 4 * h:4 * h + 4, :].rearrange("p k n -> p (k n)"), bank[i][:],
                                         ACT.Square, accum_out=stat[:, 6 + i:7 + i]).then_inc(sumsq, 1)
            act.wait_ge(rstd, 3)
            act.wait_ge(fg_ready, 4)
            nc.scalar.activation(x_sb[:, 0, :], x_sb[:, 0, :], ACT.Copy, scale=stat[:, 4:5]).then_inc(out_act, 1)

        @block.vector
        def _(dve):
            steps = [0]

            def link(ins):
                steps[0] += 1
                ins.then_inc(dve_step, 1)
                dve.wait_ge(dve_step, steps[0])

            V = nc.vector

            def mean_square():
                V.tensor_scalar(stat[:, 2:4], stat[:, 0:2], 1.0 / D, EPS, ALU.mult, ALU.add).then_inc(meansq, 1)

            dve.wait_ge(sumsq, 2)
            mean_square()
            dve.wait_ge(rstd, 1)
            for b in range(TB):
                V.tensor_scalar(xn[:, b, :], x_sb[:, b, :], stat[:, 4 + b:5 + b], None, ALU.mult).then_inc(xn_ready, 1)
            dve.wait_ge(cols_ready, 2)
            dve.wait_ge(dt_ready, 1)
            are, aim = cols[:, R_ARE:R_ARE + ST], cols[:, R_AIM:R_AIM + ST]

            def c(i):
                return s5c[:, i, :]

            V.tensor_tensor(c(1), are, dt_t[:], ALU.mult).then_inc(expo_ready, 1)
            link(V.tensor_tensor(c(3), aim, dt_t[:], ALU.mult))
            link(V.tensor_scalar(c(7), c(3), 1.0 / TWO_PI, ROUNDER, ALU.mult, ALU.add))
            link(V.tensor_scalar(c(7), c(7), ROUNDER, None, ALU.subtract))
            for part in (PI_HI, PI_MID, PI_LO):
                link(V.scalar_tensor_tensor(c(3), c(7), -part, c(3), ALU.mult, ALU.add))
            V.tensor_scalar(c(4), c(3), PI_CLAMP, -PI_CLAMP, ALU.min, ALU.max).then_inc(angle_ready, 1)
            for k in ODD_BANKS:
                dve.wait_ge(hT_psum, k - k % 2 + 2)
                V.tensor_scalar(hT[:, k, :], psum_half(8 + k), cols[:, R_GMIX + k:R_GMIX + k + 1], None, ALU.mult)\
                    .then_inc(hT_dve, 1)
            dve.wait_ge(consts, 2)
            link(V.tensor_scalar(par_i[:], par_i[:], 4, 1, ALU.logical_shift_right, ALU.bitwise_and))
            link(V.tensor_copy(par[:, 1:2], par_i[:]))
            link(V.tensor_scalar(par[:, 0:1], par[:, 1:2], -1.0, 1.0, ALU.mult, ALU.add))
            dve.wait_ge(c_in, 32)
            for i in range(2):
                for g in range(2):
                    ins = V.tensor_scalar(zc[:, i, :, g, :], cld[:, i], par[:, g:g + 1], None, ALU.mult)
            ins.then_inc(zc_ready, 1)
            link(V.tensor_tensor(c(8), are, are, ALU.mult))
            link(V.tensor_tensor(c(9), aim, aim, ALU.mult))
            link(V.tensor_tensor(c(8), c(8), c(9), ALU.add))
            link(V.reciprocal(c(9), c(8)))
            dve.wait_ge(sines_ready, 1)
            link(V.tensor_tensor(c(6), c(6), c(6), ALU.mult))
            link(V.tensor_scalar(c(6), c(6), -2.0, 1.0, ALU.mult, ALU.add))
            dve.wait_ge(rho_ready, 1)
            link(V.tensor_tensor(c(10), c(2), c(6), ALU.mult))
            link(V.tensor_scalar(c(10), c(10), 1.0, None, ALU.subtract))
            link(V.tensor_tensor(c(11), c(2), c(5), ALU.mult))
            V.tensor_tensor(c(12), c(10), are, ALU.mult)
            link(V.tensor_tensor(c(13), c(11), aim, ALU.mult))
            link(V.tensor_tensor(c(12), c(12), c(13), ALU.add))
            link(V.tensor_tensor(c(14), c(12), c(9), ALU.mult))
            V.tensor_tensor(c(12), c(11), are, ALU.mult)
            link(V.tensor_tensor(c(13), c(10), aim, ALU.mult))
            link(V.tensor_tensor(c(12), c(12), c(13), ALU.subtract))
            link(V.tensor_tensor(c(15), c(12), c(9), ALU.mult))
            dve.wait_ge(b_in, 32)
            kr = c(14).unsqueeze(2).to_broadcast([P, ST, GH])
            ki = c(15).unsqueeze(2).to_broadcast([P, ST, GH])
            V.tensor_tensor(btmp[:, 0], bld[:, 0], kr, ALU.mult)
            V.tensor_tensor(btmp[:, 1], bld[:, 1], ki, ALU.mult)
            V.tensor_tensor(btmp[:, 2], bld[:, 1], kr, ALU.mult)
            link(V.tensor_tensor(btmp[:, 3], bld[:, 0], ki, ALU.mult))
            for g in range(2):
                h = slice(64 * g, 64 * g + 64)
                V.tensor_tensor(zb[h, 0, :, GH * g:GH * g + GH], btmp[h, 0], btmp[h, 1], ALU.subtract)
                ins = V.tensor_tensor(zb[h, 1, :, GH * g:GH * g + GH], btmp[h, 2], btmp[h, 3], ALU.add)
            ins.then_inc(zb_ready, 1)

            def power(i, k, tbl):
                return tbl[:, i, :, k:k + 1]

            for tbl, first in ((lowT, None), (highT, lowT)):
                if first is None:
                    V.tensor_copy(power(0, 1, tbl), c(6).unsqueeze(2))
                    link(V.tensor_copy(power(1, 1, tbl), c(5).unsqueeze(2)))
                else:
                    r8, i8 = power(0, 8, first), power(1, 8, first)
                    V.tensor_tensor(ptmp[:, 0, :, 0:1], r8, r8, ALU.mult)
                    V.tensor_tensor(ptmp[:, 1, :, 0:1], i8, i8, ALU.mult)
                    link(V.scalar_tensor_tensor(power(1, 1, tbl), r8, 2.0, i8, ALU.mult, ALU.mult))
                    link(V.tensor_tensor(power(0, 1, tbl), ptmp[:, 0, :, 0:1], ptmp[:, 1, :, 0:1], ALU.subtract))
                n = 1
                while n < 16:
                    if n > 1:
                        r, i = power(0, n // 2, tbl), power(1, n // 2, tbl)
                        V.tensor_tensor(ptmp[:, 0, :, 0:1], r, r, ALU.mult)
                        V.tensor_tensor(ptmp[:, 1, :, 0:1], i, i, ALU.mult)
                        link(V.scalar_tensor_tensor(power(1, n, tbl), r, 2.0, i, ALU.mult, ALU.mult))
                        link(V.tensor_tensor(power(0, n, tbl), ptmp[:, 0, :, 0:1], ptmp[:, 1, :, 0:1], ALU.subtract))
                        m = n - 1
                        lo_r, lo_i = tbl[:, 0, :, 1:n], tbl[:, 1, :, 1:n]
                        pr = power(0, n, tbl).to_broadcast([P, ST, m])
                        pi = power(1, n, tbl).to_broadcast([P, ST, m])
                        t0, t1 = ptmp[:, 0, :, 0:m], ptmp[:, 1, :, 0:m]
                        V.tensor_tensor(t0, lo_r, pr, ALU.mult)
                        link(V.tensor_tensor(t1, lo_i, pi, ALU.mult))
                        link(V.tensor_tensor(tbl[:, 0, :, n + 1:2 * n], t0, t1, ALU.subtract))
                        V.tensor_tensor(t0, lo_r, pi, ALU.mult)
                        link(V.tensor_tensor(t1, lo_i, pr, ALU.mult))
                        link(V.tensor_tensor(tbl[:, 1, :, n + 1:2 * n], t0, t1, ALU.add))
                    n *= 2
            V.tensor_copy(par[:, 0:1], par[:, 1:2]).then_inc(powers_ready, 1)
            dve.wait_ge(bt_psum, 2)
            for i, (src, scale) in enumerate(((6, 1.0), (7, -1.0))):
                ins = V.tensor_scalar(CT[:, i], bank[src][:].rearrange("p (b n) -> p b n", b=YB), scale, None, ALU.mult)
            ins.then_inc(ct_ready, 1)

            def conv(j):
                s = j % 2
                w = [cols[:, R_CONVW + KD * i + j:R_CONVW + KD * i + j + 1] for i in range(3)]
                dve.wait_ge(xs_ready, j + 1)
                dve.wait_ge(xbc_psum, 3 * j + 3)
                link(V.tensor_tensor(v_sb[:, s, 2:T + 2], bank[2 * s + 1][:, T:2 * T], xs[:, s, :], ALU.mult))
                link(V.tensor_scalar(ct[:, 0, :], v_sb[:, s, 2:T + 2], w[2], cols[:, R_CONVB + j:R_CONVB + j + 1],
                                     ALU.mult, ALU.add))
                link(V.scalar_tensor_tensor(ct[:, 1, :], v_sb[:, s, 1:T + 1], w[1], ct[:, 0, :], ALU.mult, ALU.add))
                link(V.scalar_tensor_tensor(ct[:, 0, :], v_sb[:, s, 0:T], w[0], ct[:, 1, :], ALU.mult, ALU.add))
                V.tensor_tensor(z_sb[:, j, :], bank[2 * s + 1][:, 0:T], ct[:, 0, :], ALU.mult).then_inc(z_ready, 1)
                dve.wait_ge(z_ready, j + 1)

            def s5_step(t):
                b, q = t // 4, t % 4
                cos, sin = rot[:, b % 2, 0, q, :], rot[:, b % 2, 1, q, :]
                if q == 0:
                    dve.wait_ge(rot_ready, b + 1)
                dve.wait_ge(bu_psum, t + 1)
                bu = bank[4 + t % 2][:].rearrange("p (i t) -> p i t", i=2)
                cos2, sin2 = (w.unsqueeze(1).to_broadcast([P, 2, T]) for w in (cos, sin))
                V.tensor_tensor(turned[:, 0], bu, cos2, ALU.mult)
                V.tensor_tensor(turned[:, 1], bu, sin2, ALU.mult).then_inc(bu_used, 1)
                dve.wait_ge(bu_used, t + 1)
                zin, zst = turned[:, 0], turned[:, 1]
                V.tensor_tensor(zin[:, 0, :], turned[:, 0, 0, :], turned[:, 1, 1, :], ALU.add)
                link(V.tensor_tensor(zin[:, 1, :], turned[:, 0, 1, :], turned[:, 1, 0, :], ALU.subtract))
                rho = s5c[:, 2, t:t + 1].to_broadcast([P, T])
                V.tensor_tensor_scan(zst[:, 0, :], rho, zin[:, 0, :], 0.0, ALU.mult, ALU.add)
                link(V.tensor_tensor_scan(zst[:, 1, :], rho, zin[:, 1, :], 0.0, ALU.mult, ALU.add))
                if t >= 2:
                    dve.wait_ge(s_ready, t - 1)
                if t >= 4:
                    dve.wait_ge(q_used, t - t % 2 - 2)
                V.tensor_tensor(s_sb[:, t % 4], zst, cos2, ALU.mult)
                ins = V.tensor_tensor(sprod[:, t % 2], zst, sin2, ALU.mult)
                ins.then_inc(q_ready, 1)
                dve.wait_ge(q_ready, t + 1)
                if q == 3:
                    V.tensor_copy(par[:, 0:1], par[:, 1:2]).then_inc(rot_used, 1)
                    dve.wait_ge(rot_used, b + 1)

            def y_pre(b):
                dve.wait_ge(q_used, 4 * b + 4)
                V.scalar_tensor_tensor(yT[:, b, :], uT[:, b, :], cols[:, R_SSMD + b:R_SSMD + b + 1],
                                       bank[6 + b % 2][:, 0:T], ALU.mult, ALU.add).then_inc(ypre_ready, 1)

            def main(g):
                if g < 24 and g % 3 == 2:
                    conv(g // 3)
                elif 32 <= g < 40:
                    n = g - 32
                    dve.wait_ge(ga_ready, n + 1)
                    V.tensor_tensor(mixed[:, n, :], mixed[:, n, :], gate[:, n % 2, :], ALU.mult).then_inc(ga_used, 1)

            def s5(t):
                if t < ST:
                    s5_step(t)
                if t >= 6 and (t - 6) % 4 == 0:
                    y_pre((t - 6) // 4)
                if t == ST + S5_LAG - 1:
                    y_pre(YB - 1)

            for what, n in SCHEDULE:
                main(n) if what == "main" else s5(n)
            dve.wait_ge(gb_ready, KD)
            dve.wait_ge(ga_used, KD)
            for n in range(KD):
                dve.wait_ge(glu_sig, n + 1)
                dve.wait_ge(glu_psum, 2 * n + 2)
                link(V.tensor_tensor(xs[:, 0, :], bank[2 * (n % 2) + 1][:, 0:T], gate[:, n % 2, :], ALU.mult))
                link(V.tensor_tensor(xs[:, 1, :], xs[:, 0, :], z_sb[:, n, :], ALU.mult))
                V.tensor_tensor(mixed[:, n, :], mixed[:, n, :], xs[:, 1, :], ALU.add).then_inc(mixed_ready, 1)
                dve.wait_ge(mixed_ready, n + 1)
            dve.wait_ge(ffn_in, 16)
            for b in range(TB):
                dve.wait_ge(x_in_s[b], 32)
                for h in range(2):
                    xs_h = x_sb[:, b, 512 * h:512 * h + 512]
                    dve.wait_ge(wo_psum, 2 * b + h + 1)
                    V.tensor_tensor(xs_h, bank[4 + 2 * b + h][:], xs_h, ALU.add).then_inc(x2_ready, 1)
                dve.wait_ge(x2_ready, 2 * b + 2)
                V.tensor_tensor(*scaled_half(b, 1), ALU.mult).then_inc(xg_dve, 1)
            dve.wait_ge(sumsq, 4)
            mean_square()
            for k in ODD_BANKS:
                dve.wait_ge(h2T_psum, k - k % 2 + 2)
                V.tensor_copy(hT[:, k, :], psum_half(8 + k)).then_inc(hT_dve, 1)

            def per_token(ap, n):
                return ap.unsqueeze(2).to_broadcast([P, TB, n])

            def over_tokens(ap, n):
                return ap.unsqueeze(1).to_broadcast([P, TB, n])

            def rcol(i, n=NE):
                return rt[:, :, i, 0:n]

            def first_match(hot, values, best, n, tmp):
                link(V.tensor_tensor(tmp, values, per_token(best, n), ALU.is_equal))
                link(V.scalar_tensor_tensor(tmp, tmp, -64.0, over_tokens(iota[:, 0:n], n), ALU.mult, ALU.add))
                link(V.tensor_reduce(rs[:, 15, :], tmp, AX.X, ALU.min))
                link(V.tensor_tensor(hot, tmp, per_token(rs[:, 15, :], n), ALU.is_equal))

            dve.wait_ge(logits_psum, 1)
            dve.wait_ge(route_in, 64)
            logits = bank[4][:, 0:TB * (NEG + NE)].rearrange("p (b n) -> p b n", b=TB)
            dve.wait_ge(rstd, 2)
            for b in range(TB):
                r = stat[:, 4 + b:5 + b]
                V.scalar_tensor_tensor(rt[:, b, 2, 0:NEG], logits[:, b, 0:NEG], r, br[:, 0:NEG], ALU.mult, ALU.add)
                ins = V.scalar_tensor_tensor(rt[:, b, 3, :], logits[:, b, NEG:], r, br[:, NEG:], ALU.mult, ALU.add)
            link(ins)
            link(V.tensor_reduce(rs[:, 0, :], rcol(2, NEG), AX.X, ALU.max))
            V.tensor_tensor(rcol(0, NEG), rcol(2, NEG), per_token(rs[:, 0, :], NEG), ALU.subtract).then_inc(expin_ready, 1)
            first_match(rcol(4, NEG), rcol(2, NEG), rs[:, 0, :], NEG, rcol(5, NEG))
            link(V.tensor_scalar(rcol(5, NEG), rcol(4, NEG), -MASKED, MASKED, ALU.mult, ALU.add))
            for b in range(TB):
                ins = V.tensor_tensor(rt[:, b, 6, :].rearrange("p (g e) -> p g e", g=NEG),
                                      rt[:, b, 3, :].rearrange("p (g e) -> p g e", g=NEG),
                                      rt[:, b, 5, 0:NEG].unsqueeze(2).to_broadcast([P, NEG, EG]), ALU.add)
            link(ins)
            link(V.tensor_reduce(rs[:, 1, :], rcol(6), AX.X, ALU.max))
            first_match(rcol(7), rcol(6), rs[:, 1, :], NE, rcol(9))
            link(V.scalar_tensor_tensor(rcol(6), rcol(7), 3.0 * MASKED, rcol(6), ALU.mult, ALU.add))
            link(V.tensor_reduce(rs[:, 2, :], rcol(6), AX.X, ALU.max))
            V.tensor_tensor(rs[:, 8, :], rs[:, 2, :], rs[:, 1, :], ALU.subtract).then_inc(expin_ready, 1)
            first_match(rcol(8), rcol(6), rs[:, 2, :], NE, rcol(9))
            V.tensor_tensor(member[:], rcol(7), rcol(8), ALU.add).then_inc(member_ready, 1)
            dve.wait_ge(exp_ready, 2)
            V.tensor_scalar(rs[:, 10, :], rs[:, 9, :], 1.0, None, ALU.add)
            link(V.tensor_reduce(rs[:, 11, :], rcol(1, NEG), AX.X, ALU.add))
            link(V.tensor_tensor(rs[:, 12, :], rs[:, 10, :], rs[:, 11, :], ALU.mult))
            link(V.reciprocal(rs[:, 13, :], rs[:, 12, :]))
            link(V.tensor_tensor(rs[:, 14, :], rs[:, 13, :], rs[:, 9, :], ALU.mult))
            V.tensor_tensor(rcol(9), rcol(7), per_token(rs[:, 13, :], NE), ALU.mult)
            link(V.tensor_tensor(rcol(10), rcol(8), per_token(rs[:, 14, :], NE), ALU.mult))
            V.tensor_tensor(weight, rcol(9), rcol(10), ALU.add)
            link(V.tensor_scalar(rcol(11), member[:], -UNSELECTED, UNSELECTED, ALU.mult, ALU.add))
            dve.wait_ge(rank_psum, 1)
            link(V.tensor_tensor(rank, rcol(11), bank[5][:, 0:2 * NE].rearrange("p (b n) -> p b n", b=TB), ALU.add))
            link(V.tensor_reduce(cnt_f[:], bank[5][:, 2 * NE:3 * NE], AX.X, ALU.max))
            V.tensor_copy(most[:], cnt_f[:]).then_inc(most_ready, 1)

            def experts(rnd):
                with dve.Fori(0, BODIES) as it:
                    for pk in range(BODY_PACKS):
                        done = rnd * PACKS + it * BODY_PACKS + (pk + 1)
                        first = it * (BODY_PACKS * PACK) + pk * PACK
                        shape = [P, TB, PACK, SLOTS]
                        dve.wait_ge(slots_moved, rnd + 1)
                        V.tensor_tensor(sel, slot_no[:].unsqueeze(1).unsqueeze(1).to_broadcast(shape),
                                        rank[:, :, bass.ds(first, PACK)].unsqueeze(3).to_broadcast(shape),
                                        ALU.is_equal).then_inc(sel_ready, 1)
                        dve.wait_ge(sel_ready, done)
                        V.tensor_tensor(wsel, sel,
                                        weight[:, :, bass.ds(first, PACK)].unsqueeze(3).to_broadcast(shape),
                                        ALU.mult).then_inc(wsel_ready, 1)
                        dve.wait_ge(gather_psum, done * 2)
                        V.tensor_copy(xT[:, 4:8, :], bank[7][:].rearrange("p (k s) -> p k s", k=4)).then_inc(xT_dve, 1)
                        dve.wait_ge(silu_ready, done)
                        dve.wait_ge(up_psum, done)
                        V.tensor_tensor(act_sb.rearrange("p c q -> p q c"),
                                        silu.rearrange("p (q c) -> p q c", c=KF),
                                        bank[5][:].rearrange("p (q c) -> p q c", c=KF), ALU.mult).then_inc(act_ready, 1)
                        dve.wait_ge(down_psum, done)
                        V.tensor_copy(y_sb[:, 512:D], bank[7][:]).then_inc(y_dve, 1)
                V.tensor_scalar(slot_no[:], slot_no[:], float(SLOTS), None, ALU.add).then_inc(slots_moved, 1)

            experts(0)
            dve.wait_ge(most_ready, 1)
            most_r = dve.value_load(most[0:1, 0:1], min_val=0, max_val=T)
            with dve.Fori(1, ROUNDS) as rnd:
                with dve.If(most_r > rnd * SLOTS):
                    experts(rnd)
            dve.wait_ge(moe_psum, 1)
            dve.wait_ge(fin_in, 16)
            for n, (b, h) in enumerate(((1, 0), (1, 1), (0, 0), (0, 1))):
                if b == 0:
                    dve.wait_ge(sumsq, 4 + h + 1)
                half = slice(512 * h, 512 * h + 512)
                V.tensor_tensor(x_sb[:, b, half], bank[2 * b + h][:], g_fin[:, half], ALU.mult).then_inc(fg_ready, 1)
            dve.wait_ge(sumsq, 8)
            link(V.tensor_tensor(stat[:, 0:2], stat[:, 6:10:2], stat[:, 7:11:2], ALU.add))
            mean_square()
            dve.wait_ge(rstd, 3)
            V.tensor_scalar(x_sb[:, 1, :], x_sb[:, 1, :], stat[:, 5:6], None, ALU.mult).then_inc(out_dve, 1)

        @block.tensor
        def _(pe):
            MM = nc.tensor.matmul

            pe.wait_ge(consts, 1)
            pe.wait_ge(rows_in, 16 * 8)
            nc.tensor.transpose(bank[0][:, 0:N_ROWS], rows[:], ident[0:N_ROWS, 0:N_ROWS])
            MM(bank[0][:, 128:128 + GROUPS], ones[0:1, :], logdt_row[:], start=True, stop=True).then_inc(cols_psum, 1)
            for b in range(TB):
                pe.wait_ge(xn_ready, b + 1)
                for k in range(KD):
                    ins = nc.tensor.transpose(psum_half(8 + k)[:, b * P:(b + 1) * P], xn[:, b, k * P:(k + 1) * P], ident[:])
                    if b == TB - 1:
                        ins.then_inc(hT_psum, 1)
            owed = [0]

            def project(dst, w, n, rhs, done, kn=KD, arrives=None):
                for k in range(kn):
                    if arrives is not None:
                        pe.wait_ge(arrives, k + 1)
                    ins = MM(dst, w[:, k, n * P:(n + 1) * P], rhs[:, k, :], start=k == 0, stop=k == kn - 1)
                    if k == 0 and owed[0]:
                        ins.then_inc(units_used, owed[0])
                        owed[0] = 0
                return ins.then_inc(done, 1)

            mix_loaded(pe, U_U)
            for i, k in enumerate(EVEN_BANKS + ODD_BANKS):
                pe.wait_ge(*((hT_act, i + 1) if i < 4 else (hT_dve, i - 3)))
                ins = MM(psum_half(4), w8(U_U)[:, k, 0:P], hT[:, k, :], start=i == 0, stop=i == KD - 1)
            ins.then_inc(u_psum, 1)
            for n in range(1, YB):
                project(psum_half(4 + n), w8(U_U), n, hT, u_psum)
            owed[0] += 1
            pe.wait_ge(zb_ready, 1)
            for i in range(2):
                for b in range(YB):
                    ins = nc.tensor.transpose(bank[4 + i][:, b * P:(b + 1) * P],
                                              zb[:, i, 4 * b:4 * b + 4, :].rearrange("p t h -> p (t h)"), ident[:])
            ins.then_inc(bt_psum, 1)
            pe.wait_ge(zc_ready, 1)
            for i in range(2):
                for b in range(YB):
                    ins = nc.tensor.transpose(bank[6 + i][:, b * P:(b + 1) * P],
                                              zc[:, i, b].rearrange("p g n -> p (g n)"), ident[:])
            ins.then_inc(bt_psum, 1)

            def main(g):
                if g < 24:
                    j, part = g // 3, g % 3
                    unit = U_XBC + 3 * (j // 4) + part
                    if g == 0:
                        pe.wait_ge(cols_ready, 2)
                    if g == 3:
                        pe.wait_ge(u_ready, YB)
                    if part == 0 and j >= 2:
                        pe.wait_ge(z_ready, j - 1)
                    mix_loaded(pe, unit)
                    s = 2 * (j % 2)
                    dst = (bank[s][:, 0:T], bank[s + 1][:, 0:T], bank[s + 1][:, T:2 * T])[part]
                    project(dst, w8(unit), j % 4, hT, xbc_psum)
                elif g < 32:
                    n = g - 24
                    if n <= 1:
                        pe.wait_ge(z_ready, KD - 1 + n)
                    if n >= 4:
                        pe.wait_ge(ya_ready, n - 3)
                    mix_loaded(pe, U_CO + n // 4)
                    project(bank[n % 4][:, 0:T], w8(U_CO + n // 4), n % 4, z_sb, ya_psum, arrives=z_ready if n == 0 else None)
                elif g < 40:
                    n = g - 32
                    pe.wait_ge(*((ya_ready, n + 5) if n < 4 else (ga_ready, n - 3)))
                    mix_loaded(pe, U_GA + n // 4)
                    project(bank[n % 4][:, 0:T], w8(U_GA + n // 4), n % 4, hT, ga_psum)
                else:
                    n = g - 40
                    pe.wait_ge(*((ga_ready, n + 5) if n < 4 else (gb_ready, n - 3)))
                    mix_loaded(pe, U_GB + n // 4)
                    project(bank[n % 4][:, 0:T], w8(U_GB + n // 4), n % 4, hT, gb_psum)
                if g in (11, 23):
                    owed[0] += 3
                if g >= 24 and g % 4 == 3:
                    owed[0] += 1

            def s5(t):
                if t < ST and t % 2 == 0:
                    b, q = t // 4, t % 4
                    if t == 0:
                        pe.wait_ge(bt_ready, 1)
                        pe.wait_ge(u_ready, YB)
                    if t >= 2:
                        pe.wait_ge(bu_used, t)
                    for i in range(2):
                        for n in range(2):
                            r = slice(32 * (q + n), 32 * (q + n) + 32)
                            ins = MM(bank[4 + n][:, i * T:(i + 1) * T], BT[r, b, i, :], uT[r, b, :],
                                     start=True, stop=True)
                    ins.then_inc(bu_psum, 2)
                if t > S5_LAG and t % 2:
                    t -= S5_LAG + 1
                    b, q = t // 4, t % 4
                    if t == 0:
                        pe.wait_ge(ct_ready, 1)
                    if q == 0 and b >= 2:
                        pe.wait_ge(ypre_ready, b - 1)
                    pe.wait_ge(s_ready, t + 2)
                    for i in range(2):
                        for n in range(2):
                            c = slice(32 * (q + n), 32 * (q + n) + 32)
                            ins = MM(bank[6 + b % 2][c, 0:T], CT[:, i, b, c], s_sb[:, (t + n) % 4, i, :],
                                     start=i == 0, stop=i == 1)
                    ins.then_inc(q_used, 2)

            for what, n in SCHEDULE:
                main(n) if what == "main" else s5(n)

            def project_out(k):
                pe.wait_ge(mixed_ready, k + 1)
                mix_loaded(pe, U_WO + k // 4)
                for b in range(TB):
                    for h in range(2):
                        ins = MM(bank[4 + 2 * b + h][:], mixed[:, k, b * P:(b + 1) * P],
                                 w4(U_WO + k // 4)[:, k % 4, 512 * h:512 * h + 512], start=k == 0, stop=k == KD - 1)
                        if k == KD - 1:
                            ins.then_inc(wo_psum, 1)

            pe.wait_ge(y_ready, YB)
            pe.wait_ge(gb_ready, KD)
            for n in range(KD):
                if n >= 2:
                    pe.wait_ge(mixed_ready, n - 1)
                for i, unit in enumerate((U_GLUB, U_GLUA)):
                    mix_loaded(pe, unit)
                    project(bank[2 * (n % 2) + i][:, 0:T], w4(unit), n, yT, glu_psum, YB)
                if n == KD - 1:
                    pe.wait_ge(glu_psum, 2 * KD)
                    pe.sem_inc(units_used, 3)
                if n >= 1:
                    project_out(n - 1)
            project_out(KD - 1)
            pe.wait_ge(wo_psum, 2 * TB)
            pe.sem_inc(units_used, 1)

            for b in range(TB):
                for h in range(2):
                    pe.wait_ge(x2_ready, 2 * b + h + 1)
                    MM(bank[2 * b + h][:], ident[:], x_sb[:, b, 512 * h:512 * h + 512], start=True, stop=True)
            for b in range(TB):
                pe.wait_ge(xg_pool, b + 1)
                pe.wait_ge(xg_dve, b + 1)
                for k in range(KD):
                    ins = nc.tensor.transpose(psum_half(8 + k)[:, b * P:(b + 1) * P], h2[:, b, k, :], ident[:])
                    if b == TB - 1:
                        ins.then_inc(h2T_psum, 1)
            pe.wait_ge(hT_act, KD)
            pe.wait_ge(hT_dve, KD)
            pe.wait_ge(route_in, 64)
            for b in range(TB):
                n = NEG + NE
                for k in range(KD):
                    ins = MM(bank[4][:, b * n:(b + 1) * n], hT[:, k, b * P:(b + 1) * P], wr[:, k, :],
                             start=k == 0, stop=k == KD - 1)
            ins.then_inc(logits_psum, 1)
            pe.wait_ge(member_ready, 1)
            MM(bank[5][:, 0:NE], upper16[:], member[:, 0, :], start=True, stop=True)
            MM(bank[5][:, NE:2 * NE], ones16[:], member[:, 0, :], start=True, stop=False)
            MM(bank[5][:, NE:2 * NE], upper16[:], member[:, 1, :], start=False, stop=True)
            MM(bank[5][:, 2 * NE:3 * NE], ones16[:], member[:, 0, :], start=True, stop=False)
            MM(bank[5][:, 2 * NE:3 * NE], ones16[:], member[:, 1, :], start=False, stop=True).then_inc(rank_psum, 1)

            def experts(rnd):
                with pe.Fori(0, BODIES) as it:
                    for pk in range(BODY_PACKS):
                        expert_pack(rnd, it, pk)

            def expert_pack(rnd, it, pk):
                done = rnd * PACKS + it * BODY_PACKS + (pk + 1)

                def unit(w):
                    v = pk * PACK_UNITS + w
                    u = MIX_UNITS + v
                    bodies = rnd * BODIES + it
                    if v < len(extra):
                        pe.wait_ge(extra_in[v], (bodies + 1) * 16)
                        return extra[v].rearrange("p (e n) -> p e n", e=PACK)
                    slot = u % RING
                    per_body = BODY_UNITS // RING - (slot in SKIPPED)
                    fills = bodies * per_body + (u // RING + 1 - (slot in SKIPPED))
                    pe.wait_ge(loaded[slot], fills * 16)
                    return ring[:, slot, :].rearrange("p (e n) -> p e n", e=PACK)

                pe.wait_ge(sel_ready, done)
                if pk == 0:
                    pe.wait_ge(h2_ready, TB)
                for k in range(KD):
                    for b in range(TB):
                        ins = MM(bank[6 + k // 4][:, (k % 4) * P:(k % 4 + 1) * P], h2[:, b, k, :],
                                 sel[:, b].rearrange("p e s -> p (e s)"), start=b == 0, stop=b == TB - 1)
                    if k % 4 == 3:
                        ins.then_inc(gather_psum, 1)
                pe.wait_ge(wsel_ready, done)
                for b in range(TB):
                    ins = nc.tensor.transpose(bank[5][:, b * P:(b + 1) * P],
                                              wsel[:, b].rearrange("p e s -> p (e s)"), ident[:])
                ins.then_inc(wselT_psum, 1)
                pe.wait_ge(xT_act, done)
                for w in range(8):
                    if w == 1:
                        pe.wait_ge(wselT_ready, done)
                    if w == 4:
                        pe.wait_ge(xT_dve, done)
                    wt = unit(w)
                    for kk in range(2):
                        k = 2 * (w // 2) + kk
                        for e in range(PACK):
                            q = slice(SLOTS * e, SLOTS * e + SLOTS)
                            ins = MM(bank[4 + w % 2][q, :], xT[:, k, q], wt[:, e, 512 * kk:512 * kk + 512],
                                     start=k == 0, stop=k == KD - 1)
                    if w < 7:
                        ins.then_inc(units_used, 1)
                    else:
                        ins.then_inc(up_psum, 1)
                pe.wait_ge(up_psum, done)
                pe.sem_inc(units_used, 1)
                pe.wait_ge(act_ready, done)
                for c in range(KF):
                    ins = nc.tensor.transpose(bank[4][:, c * P:(c + 1) * P], act_sb[:, c, :], ident[:])
                ins.then_inc(actT_psum, 1)
                pe.wait_ge(actT_ready, done)
                for c in range(KF):
                    wt = unit(8 + c)
                    for h in range(2):
                        for e in range(PACK):
                            q = slice(SLOTS * e, SLOTS * e + SLOTS)
                            ins = MM(bank[6 + h][q, :], actT[:, c, q], wt[:, e, 512 * h:512 * h + 512],
                                     start=c == 0, stop=c == KF - 1)
                    if c < KF - 1:
                        ins.then_inc(units_used, 1)
                    else:
                        ins.then_inc(down_psum, 1)
                pe.wait_ge(down_psum, done)
                pe.sem_inc(units_used, 1)
                pe.wait_ge(y_act, done)
                pe.wait_ge(y_dve, done)
                for b in range(TB):
                    for h in range(2):
                        MM(bank[2 * b + h][:], wselT[:, b, :], y_sb[:, 512 * h:512 * h + 512],
                           start=False, stop=True, skip_group_check=True)

            experts(0)
            pe.wait_ge(most_ready, 1)
            most_r = pe.value_load(most[0:1, 0:1], min_val=0, max_val=T)
            with pe.Fori(1, ROUNDS) as rnd:
                with pe.If(most_r > rnd * SLOTS):
                    experts(rnd)
            MM(bank[4][:, 0:4], ident[:], ident[:, 0:4], start=True, stop=True).then_inc(moe_psum, 1)


_INS = ["x", "norm_mix", "w_in", "conv_w", "conv_b", "w_conv_out", "ssm_a_re", "ssm_a_im", "ssm_log_dt",
        "ssm_b_re", "ssm_b_im", "ssm_c_re", "ssm_c_im", "ssm_d", "w_glu_a", "w_glu_b", "gate_bias", "w_o",
        "norm_ffn", "w_route_group", "b_route_group", "w_route_expert", "b_route_expert", "w_gate", "w_up",
        "w_down", "norm_final"]


def kernel(**inputs):
    import numpy as np
    import concourse.bacc as bacc
    from concourse.bass_utils import run_bass_kernel_spmd

    nc = bacc.Bacc("TRN2", target_bir_lowering=False, num_devices=1, dynamic_dma_scratch_size=1024)
    arrays, args = {}, []
    for name in _INS:
        a = np.ascontiguousarray(inputs[name])
        arrays[f"in_{name}"] = a
        args.append(nc.dram_tensor(f"in_{name}", a.shape, mybir.dt.from_np(a.dtype), kind="ExternalInput").ap())
    args.append(nc.dram_tensor("out_dram", (1, T, D), mybir.dt.float32, kind="ExternalOutput").ap())
    block_kernel(nc, *args)
    r = run_bass_kernel_spmd(nc, [arrays], core_ids=[0])
    return r.results[0]["out_dram"]
```

```python
from contextlib import ExitStack

import concourse.bass as bass
from concourse import mybir

D = 1024
T = 256
P = 128
KD = D // P
TB = T // P
SSM = 512
YB = SSM // P
GROUPS, STATE, GH = 32, 64, 16
ST = GROUPS * STATE // P
NEG, EG, NE = 4, 8, 32
FF = 512
KF = FF // P
EPS = 1e-6

UNIT = 4096
RING = 8
MIX_UNITS = 17
SLOTS = 32
PACK = P // SLOTS
PACKS = NE // PACK
PACK_UNITS = 12
BODY_PACKS = 2
BODY_UNITS = BODY_PACKS * PACK_UNITS
BODIES = PACKS // BODY_PACKS
ROUNDS = T // SLOTS
UNSELECTED = 1.0e4

TWO_PI = 6.283185307179586
PI_HI, PI_MID = 6.28125, 0.0019350051879882812
PI_LO = TWO_PI - PI_HI - PI_MID
ROUNDER = 12582912.0
PI_CLAMP = 3.1415925
EULER = 2.718281828459045
MASKED = -1.0e30

R_GMIX, R_ARE, R_AIM, FIRST_ROWS = 0, 8, 24, slice(0, 40)
R_CONVW, R_CONVB, R_GATEB, R_SSMD, LATER_ROWS = 64, 88, 96, 112, slice(64, 116)
N_ROWS = 116

EVEN_BANKS, ODD_BANKS = (0, 1, 4, 5), (2, 3, 6, 7)

N_MAIN = 48
N_LOGITS = NEG + NE
S5_LAG = 2


def mixer_schedule():
    order, step = [], 0
    for g in range(N_MAIN):
        order.append(("main", g))
        if g >= 4 and g % 2 == 0 and step < ST + S5_LAG:
            order.append(("s5", step))
            step += 1
    while step < ST + S5_LAG:
        order.append(("s5", step))
        step += 1
    return order


def block_kernel(nc, x_in, norm_mix, w_in, conv_w, conv_b, w_conv_out, a_re, a_im, log_dt, b_re, b_im,
                 c_re, c_im, ssm_d, w_glu_a, w_glu_b, gate_bias, w_o, norm_ffn, w_rg, b_rg, w_re, b_re_,
                 w_gate, w_up, w_down, norm_final, out):
    f32 = mybir.dt.float32
    i32 = mybir.dt.int32
    bf16 = mybir.dt.bfloat16
    ALU = mybir.AluOpType
    ACT = mybir.ActivationFunctionType
    AX = mybir.AxisListType
    SCHEDULE = mixer_schedule()

    ctx = ExitStack()
    with ctx:
        def sb(name, shape, dt=f32):
            return ctx.enter_context(nc.sbuf_tensor(name, shape, dt))

        def sem(name):
            return ctx.enter_context(nc.semaphore(name))

        ring = sb("ring", [P, RING, UNIT])
        rows = sb("rows", [N_ROWS, P])
        cols = sb("cols", [P, 128])
        logdt_row = sb("logdt_row", [1, GROUPS])
        ident = sb("ident", [P, P])
        ones = sb("ones", [P, P])
        s5c = sb("s5c", [P, 16, ST])
        dt_t = sb("dt_t", [P, ST])
        eul = sb("eul", [P, ST])
        par_i = sb("par_i", [P, 1], i32)
        par = sb("par", [P, 2])
        ptmp = sb("ptmp", [P, 2, ST, 8])
        stat = sb("stat", [P, 12])
        halfneg = sb("halfneg", [P, 2])
        minus_one = sb("minus_one", [P, TB])
        wr = sb("wr", [P, KD, NEG + NE])
        br = sb("br", [P, NEG + NE])
        rs = sb("rs", [P, 16, TB])
        from_end = sb("from_end", [P, NE])
        slot_no = sb("slot_no", [P, SLOTS])
        member = sb("member", [P, TB, NE], bf16)
        upper16 = sb("upper16", [P, P], bf16)
        ones16 = sb("ones16", [P, P], bf16)
        cnt_f = sb("cnt_f", [P, 1])
        most = sb("most", [P, 1], i32)

        def region(name, n):
            flat = sb(name, [P, n])

            def view(at, *shape):
                size = 1
                for d in shape:
                    size *= d
                assert at + size <= n
                names = "abcd"[:len(shape)]
                form = f"p ({' '.join(names)}) -> p {' '.join(names)}"
                return flat[:, at:at + size].rearrange(form, **dict(zip(names, shape)))
            return view

        x_region = region("x_region", UNIT)
        hT = x_region(TB * D, KD, T)
        x_sb = x_region(0, TB, D)
        rtmp = x_region(0, 4, T)
        turned = x_region(4 * T, 2, 2, T)
        extra2 = x_region(0, UNIT)
        h2_region = region("h2_region", TB * D)
        zb = h2_region(0, 2, ST, 2 * GH)
        zc = h2_region(D, 2, YB, 2, STATE)
        s_sb = h2_region(0, 4, 2, T)
        h2 = h2_region(0, TB, KD, P)
        m_region = region("m_region", KD * T)
        xn = m_region(0, TB, D)
        mixed = m_region(0, KD, T)
        y_sb = m_region(0, D)
        actT = m_region(D, KF, P)
        z_region = region("z_region", KD * T)
        bld = z_region(0, 2, ST, GH)
        btmp = z_region(512, 4, ST, GH)
        cld = z_region(1536, 2, YB, STATE)
        z_sb = z_region(0, KD, T)
        xT = z_region(0, KD, P)
        silu = z_region(1024, FF)
        act_sb = z_region(1536, KF, P)
        u_region = region("u_region", D)
        uT = u_region(0, YB, T)
        g_ffn = u_region(0, D)
        y_region = region("y_region", D)
        yT = y_region(0, YB, T)
        g_fin = y_region(0, D)
        conv_region = region("conv_region", 8 * T + 8)
        xs = conv_region(0, 2, T)
        v_sb = conv_region(2 * T, 2, T + 2)
        ct = conv_region(4 * T + 4, 2, T)
        gate = conv_region(6 * T + 4, 2, T)
        rt = conv_region(0, TB, 12, NE)
        lg = rt[:, :, 2:4, :].rearrange("p b i n -> p b (i n)")[:, :, 0:N_LOGITS]
        lgT = conv_region(768, T)[0:N_LOGITS, :]
        sel = conv_region(768, TB, PACK, SLOTS)
        wsel = conv_region(1024, TB, PACK, SLOTS)
        wselT = conv_region(1280, TB, P)
        weight = conv_region(1536, TB, NE)
        rank = conv_region(1600, TB, NE)
        s5_region = region("s5_region", UNIT)
        BT = s5_region(0, YB, 2, P)
        CT = s5_region(1024, 2, YB, P)
        sprod = s5_region(2048, 2, 2, T)
        lowT = s5_region(3072, 2, ST, 16)
        highT = s5_region(3584, 2, ST, 16)
        extra1 = s5_region(0, UNIT)
        rot_region = region("rot_region", UNIT)
        rot = rot_region(0, 2, 2, 4, T)
        extra0 = rot_region(0, UNIT)

        bank = [ctx.enter_context(nc.psum_tensor(f"bank{i}", [P, 512], f32)) for i in range(8)]

        loaded = [sem(f"loaded{i}") for i in range(RING)]
        extra_in = [sem(f"extra_in{i}") for i in range(3)]
        units_used = sem("units_used")
        expert_units = sem("expert_units")
        x_in_s = [sem(f"x_in{i}") for i in range(TB)]
        rows_in = sem("rows_in")
        later_rows_in = sem("later_rows_in")
        b_in = sem("b_in")
        c_in = sem("c_in")
        route_in = sem("route_in")
        ffn_in = sem("ffn_in")
        fin_in = sem("fin_in")
        consts = sem("consts")
        pool_step = sem("pool_step")
        act_step = sem("act_step")
        dve_step = sem("dve_step")
        sumsq = sem("sumsq")
        meansq = sem("meansq")
        rstd = sem("rstd")
        xn_ready = sem("xn_ready")
        cols_psum = sem("cols_psum")
        cols_ready = sem("cols_ready")
        dt_ready = sem("dt_ready")
        hT_psum = sem("hT_psum")
        hT_act = sem("hT_act")
        hT_dve = sem("hT_dve")
        u_psum = sem("u_psum")
        u_ready = sem("u_ready")
        expo_ready = sem("expo_ready")
        rho_ready = sem("rho_ready")
        angle_ready = sem("angle_ready")
        sines_ready = sem("sines_ready")
        zb_ready = sem("zb_ready")
        zc_ready = sem("zc_ready")
        bt_psum = sem("bt_psum")
        bt_ready = sem("bt_ready")
        ct_ready = sem("ct_ready")
        powers_ready = sem("powers_ready")
        rot_ready = sem("rot_ready")
        rot_used = sem("rot_used")
        bu_psum = sem("bu_psum")
        bu_used = sem("bu_used")
        q_ready = sem("q_ready")
        s_ready = sem("s_ready")
        q_used = sem("q_used")
        ypre_ready = sem("ypre_ready")
        y_ready = sem("y_ready")
        xbc_psum = sem("xbc_psum")
        xs_ready = sem("xs_ready")
        z_ready = sem("z_ready")
        ya_psum = sem("ya_psum")
        ya_ready = sem("ya_ready")
        ga_psum = sem("ga_psum")
        ga_ready = sem("ga_ready")
        ga_used = sem("ga_used")
        gb_psum = sem("gb_psum")
        gb_ready = sem("gb_ready")
        glu_psum = sem("glu_psum")
        glu_sig = sem("glu_sig")
        mixed_ready = sem("mixed_ready")
        wo_psum = sem("wo_psum")
        x2_ready = sem("x2_ready")
        xg_dve = sem("xg_dve")
        xg_pool = sem("xg_pool")
        h2_ready = sem("h2_ready")
        h2T_psum = sem("h2T_psum")
        lgT_psum = sem("lgT_psum")
        lgT_ready = sem("lgT_ready")
        logits_psum = sem("logits_psum")
        residual_psum = sem("residual_psum")
        group_sum = sem("group_sum")
        weight_ready = sem("weight_ready")
        expin_ready = sem("expin_ready")
        exp_ready = sem("exp_ready")
        member_ready = sem("member_ready")
        rank_psum = sem("rank_psum")
        most_ready = sem("most_ready")
        sel_ready = sem("sel_ready")
        wsel_ready = sem("wsel_ready")
        gather_psum = sem("gather_psum")
        wselT_psum = sem("wselT_psum")
        wselT_ready = sem("wselT_ready")
        xT_act = sem("xT_act")
        xT_dve = sem("xT_dve")
        up_psum = sem("up_psum")
        silu_ready = sem("silu_ready")
        act_ready = sem("act_ready")
        actT_psum = sem("actT_psum")
        actT_ready = sem("actT_ready")
        down_psum = sem("down_psum")
        y_act = sem("y_act")
        y_dve = sem("y_dve")
        slots_moved = sem("slots_moved")
        moe_psum = sem("moe_psum")
        fg_ready = sem("fg_ready")
        out_act = sem("out_act")
        out_dve = sem("out_dve")
        stored = sem("stored")

        EXTRAS = 3
        order = [RING, RING + 1] + [(MIX_UNITS + i) % RING for i in range(RING)] + [RING + 2]
        SLOT_OF = order + order + order[4:4 + BODY_UNITS - 2 * len(order)]
        slots = [(ring[:, i, :], loaded[i]) for i in range(RING)]
        slots += list(zip((extra0, extra1, extra2), extra_in))

        def last_in_slot(v):
            earlier = [w for w in range(v) if SLOT_OF[w] == SLOT_OF[v]]
            later = [w for w in range(BODY_UNITS) if SLOT_OF[w] == SLOT_OF[v]]
            return earlier[-1] if earlier else later[-1] - BODY_UNITS

        def mix_slot(u):
            return ring[:, u % RING, :]

        def transfers_to(slot, units):
            return sum(2 if u in U_GLU else 1 for u in units if u % RING == slot)

        def mix_loaded(eng, u):
            eng.wait_ge(loaded[u % RING], 16 * transfers_to(u % RING, range(u + 1)))

        def w8(u):
            return mix_slot(u).rearrange("p (k n) -> p k n", k=KD)

        def w4(u):
            return mix_slot(u).rearrange("p (k n) -> p k n", k=4)

        U_U, U_XBC, U_CO, U_GA, U_GB, U_GLU, U_WO = 0, 1, 7, 9, 11, (13, 15), (14, 16)

        def glu_half(u):
            return mix_slot(u).rearrange("p (i k n) -> p i k n", i=2, k=4)

        def psum_half(i):
            return bank[i // 2][:, (i % 2) * T:(i % 2) * T + T]

        def scaled_half(b, h):
            half = slice(512 * h, 512 * h + 512)
            return (h2[:, b, :, 64 * h:64 * h + 64].rearrange("p k q -> p q k"),
                    x_sb[:, b, half].rearrange("p (q k) -> p q k", k=KD),
                    g_ffn[:, half].rearrange("p (q k) -> p q k", k=KD))

        GATHER_PARTS, GATHER_BANKS = ((0, 1), (2, 3, 4), (5, 6, 7)), (4, 6, 7)

        def gathered(part):
            ks = GATHER_PARTS[part]
            return (xT[:, ks[0]:ks[-1] + 1, :],
                    bank[GATHER_BANKS[part]][:, 0:len(ks) * P].rearrange("p (k s) -> p k s", k=len(ks)))

        block = ctx.enter_context(nc.Block())

        @block.sync
        def _(sp):
            def in_cols(c0):
                return w_in[0].rearrange("(k p) n -> p k n", p=P)[:, :, c0:c0 + 512]

            xbc = [in_cols(part * D + half * 512) for half in range(2) for part in range(3)]
            co = w_conv_out[0].rearrange("(k p) n -> p k n", p=P)
            wo = w_o[0].rearrange("(k p) n -> p k n", p=P)
            sources = [in_cols(3 * D)] + xbc + [co[:, :, 0:512], co[:, :, 512:D]]
            sources += [in_cols(3 * D + SSM + i * 512) for i in range(4)]
            glu = [w[0].rearrange("(k p) n -> p k n", p=P) for w in (w_glu_b, w_glu_a)]
            for h in range(2):
                sources += [[w[:, :, 512 * h:512 * h + 512] for w in glu], wo[:, 4 * h:4 * h + 4, :]]
            assert len(sources) == MIX_UNITS
            def load_rows(vectors, landed):
                for r, n, src in vectors:
                    sp.dma_start(rows[r:r + n, :], src.rearrange("(r c) -> r c", c=P)).then_inc(landed, 16)

            load_rows(((R_GMIX, KD, norm_mix[0]), (R_ARE, ST, a_re[0].rearrange("g n -> (g n)")),
                       (R_AIM, ST, a_im[0].rearrange("g n -> (g n)"))), rows_in)
            sp.dma_start(logdt_row[:], log_dt[0:1, :]).then_inc(rows_in, 16)
            for u, src in enumerate(sources):
                if u == 1:
                    load_rows(((R_CONVW, 3 * KD, conv_w[0].rearrange("a b c -> (a b c)")), (R_CONVB, KD, conv_b[0]),
                               (R_GATEB, 2 * KD, gate_bias[0].rearrange("a c -> (a c)")),
                               (R_SSMD, YB, ssm_d[0])), later_rows_in)
                    for i, part in enumerate((b_re, b_im)):
                        sp.dma_start(bld[:, i], part[0].rearrange("(t g) n h -> (g n) t h", g=2)).then_inc(b_in, 16)
                    for i, part in enumerate((c_re, c_im)):
                        sp.dma_start(cld[:, i], part[0].rearrange("(b g) h n -> (g h) b n", g=8)).then_inc(c_in, 16)
                if u == 5:
                    sp.dma_start(wr[:, :, 0:NEG], w_rg[0].rearrange("(p k) n -> p k n", p=P)).then_inc(route_in, 16)
                    sp.dma_start(wr[:, :, NEG:], w_re[0].rearrange("(p k) n -> p k n", p=P)).then_inc(route_in, 16)
                    sp.dma_start(br[:, 0:NEG], b_rg.to_broadcast([P, NEG])).then_inc(route_in, 16)
                    sp.dma_start(br[:, NEG:], b_re_.to_broadcast([P, NE])).then_inc(route_in, 16)
                if u >= RING:
                    sp.wait_ge(units_used, u - RING + 1)
                if u in U_GLU:
                    for i in range(2):
                        sp.dma_start(glu_half(u)[:, i], src[i]).then_inc(loaded[u % RING], 16)
                else:
                    sp.dma_start(mix_slot(u).rearrange("p (k n) -> p k n", k=src.shape[1]), src).then_inc(loaded[u % RING], 16)

            gate_v = w_gate[0].rearrange("e (p k) n -> p e (k n)", p=P)
            up_v = w_up[0].rearrange("e (p k) n -> p e (k n)", p=P)
            down_v = w_down[0].rearrange("e (p c) n -> p e (c n)", p=P)

            def load_round(bodies_before):
                with sp.Fori(0, BODIES) as it:
                    for v in range(BODY_UNITS):
                        pk, w = v // PACK_UNITS, v % PACK_UNITS
                        dst, landed = slots[SLOT_OF[v]]
                        first = it * (BODY_PACKS * PACK) + pk * PACK
                        last = last_in_slot(v)
                        if SLOT_OF[v] == RING + 2 and last < 0:
                            sp.wait_ge(residual_psum, 1)
                            sp.wait_ge(h2_ready, TB)
                        elif last < 0 and SLOT_OF[v] < RING:
                            sp.wait_ge(units_used, MIX_UNITS - RING + v - 1)
                        sp.wait_ge(expert_units, (bodies_before + it + 1) * BODY_UNITS + (last + 1))
                        if w < 8:
                            view = gate_v if w % 2 == 0 else up_v
                            src = view[:, bass.ds(first, PACK), (w // 2) * 1024:(w // 2 + 1) * 1024]
                        else:
                            src = down_v[:, bass.ds(first, PACK), (w - 8) * D:(w - 7) * D]
                        sp.dma_start(dst.rearrange("p (e n) -> p e n", e=PACK), src).then_inc(landed, 16)

            sp.wait_ge(s_ready, ST)
            sp.wait_ge(q_used, ST)
            load_round(0)
            sp.wait_ge(most_ready, 1)
            most_r = sp.value_load(most[0:1, 0:1], min_val=0, max_val=T)
            with sp.If(most_r > SLOTS):
                with sp.Fori(1, ROUNDS) as rnd:
                    with sp.If(most_r > rnd * SLOTS):
                        load_round(rnd * BODIES)
            for h in range(2):
                half = slice(512 * h, 512 * h + 512)
                sp.wait_ge(out_dve, h + 1)
                sp.dma_start(out[0, 0:P, half], x_sb[:, 0, half]).then_inc(stored, 16)
            sp.wait_ge(out_dve, 3)
            sp.wait_ge(out_act, 1)
            sp.dma_start(out[0, P:T, :], x_sb[:, 1, :]).then_inc(stored, 16)
            sp.wait_ge(stored, 16 * 3)

        @block.gpsimd
        def _(pool):
            steps = [0]

            def link(ins):
                steps[0] += 1
                ins.then_inc(pool_step, 1)
                pool.wait_ge(pool_step, steps[0])

            nc.gpsimd.memset(halfneg[:], -0.5)
            nc.gpsimd.memset(minus_one[:], -1.0)
            nc.gpsimd.memset(eul[:], EULER)
            nc.gpsimd.memset(ones[:], 1.0)
            nc.gpsimd.memset(ones16[:], 1.0)
            nc.gpsimd.memset(zb, 0.0)
            nc.gpsimd.memset(v_sb, 0.0)
            nc.gpsimd.memset(lowT[:, 1], 0.0)
            nc.gpsimd.memset(highT[:, 1], 0.0)
            nc.gpsimd.memset(lowT[:, 0], 1.0)
            nc.gpsimd.memset(highT[:, 0], 1.0)
            link(nc.gpsimd.memset(ident[:], 0.0))
            nc.gpsimd.affine_select(out=ident[:], in_=ident[:], compare_op=ALU.not_equal, fill=1.0, base=0,
                                    pattern=[[-1, P]], channel_multiplier=1).then_inc(consts, 1)
            nc.gpsimd.affine_select(out=upper16[:], in_=ones[:], compare_op=ALU.is_gt, fill=0.0, base=0,
                                    pattern=[[1, P]], channel_multiplier=-1)
            nc.gpsimd.iota(from_end[:], pattern=[[-1, NE]], base=NE, channel_multiplier=0,
                           allow_small_or_imprecise_dtypes=True)
            nc.gpsimd.iota(slot_no[:], pattern=[[1, SLOTS]], base=0, channel_multiplier=0,
                           allow_small_or_imprecise_dtypes=True).then_inc(slots_moved, 1)
            nc.gpsimd.iota(par_i[:], pattern=[[0, 1]], base=0, channel_multiplier=1).then_inc(consts, 1)
            pool.wait_ge(meansq, 1)
            nc.gpsimd.tensor_tensor(stat[:, 4:6], stat[:, 2:4], halfneg[:], ALU.pow).then_inc(rstd, 1)
            pool.wait_ge(cols_ready, 2)
            nc.gpsimd.tensor_tensor(dt_t[:], eul[:], s5c[:, 0, :], ALU.pow).then_inc(dt_ready, 1)
            pool.wait_ge(expo_ready, 1)
            nc.gpsimd.tensor_tensor(s5c[:, 2, :], eul[:], s5c[:, 1, :], ALU.pow).then_inc(rho_ready, 1)
            pool.wait_ge(powers_ready, 1)

            def rotations(b):
                if b >= 2:
                    pool.wait_ge(rot_used, b - 1)
                lo = [lowT[:, i, 4 * b:4 * b + 4, :].unsqueeze(2).to_broadcast([P, 4, 16, 16]) for i in range(2)]
                hi = [highT[:, i, 4 * b:4 * b + 4, :].unsqueeze(3).to_broadcast([P, 4, 16, 16]) for i in range(2)]
                o = [rot[:, b % 2, i].rearrange("p t (h l) -> p t h l", l=16) for i in range(2)]
                tmp = rtmp.rearrange("p t (h l) -> p t h l", l=16)
                nc.gpsimd.tensor_tensor(o[0], lo[0], hi[0], ALU.mult)
                link(nc.gpsimd.tensor_tensor(tmp, lo[1], hi[1], ALU.mult))
                link(nc.gpsimd.tensor_tensor(o[0], o[0], tmp, ALU.subtract))
                nc.gpsimd.tensor_tensor(o[1], lo[0], hi[1], ALU.mult)
                link(nc.gpsimd.tensor_tensor(tmp, lo[1], hi[0], ALU.mult))
                nc.gpsimd.tensor_tensor(o[1], o[1], tmp, ALU.add).then_inc(rot_ready, 1)
                pool.wait_ge(rot_ready, b + 1)

            def state_sums(t):
                s, sp = s_sb[:, t % 4], sprod[:, t % 2]
                pool.wait_ge(q_ready, t + 1)
                nc.gpsimd.tensor_tensor(s[:, 0, :], s[:, 0, :], sp[:, 1, :], ALU.subtract)
                nc.gpsimd.tensor_tensor(s[:, 1, :], s[:, 1, :], sp[:, 0, :], ALU.add).then_inc(s_ready, 1)

            rotations(0)
            rotations(1)
            for t in range(ST):
                state_sums(t)
                if t % 4 == 3 and t // 4 + 2 < YB:
                    rotations(t // 4 + 2)
            def route_weights():
                pool.wait_ge(exp_ready, 2)
                link(nc.gpsimd.tensor_scalar(rs[:, 10, :], rs[:, 9, :], 1.0, None, ALU.add))
                pool.wait_ge(group_sum, 1)
                link(nc.gpsimd.tensor_tensor(rs[:, 12, :], rs[:, 10, :], rs[:, 11, :], ALU.mult))
                link(nc.gpsimd.tensor_tensor(rs[:, 13, :], rs[:, 12, :], minus_one[:], ALU.pow))
                link(nc.gpsimd.tensor_tensor(rs[:, 14, :], rs[:, 13, :], rs[:, 9, :], ALU.mult))
                pool.wait_ge(member_ready, 1)
                nc.gpsimd.tensor_tensor(rt[:, :, 9, :], rt[:, :, 7, :], rs[:, 13, :].unsqueeze(2).to_broadcast([P, TB, NE]), ALU.mult)
                link(nc.gpsimd.tensor_tensor(rt[:, :, 10, :], rt[:, :, 8, :], rs[:, 14, :].unsqueeze(2).to_broadcast([P, TB, NE]), ALU.mult))
                nc.gpsimd.tensor_tensor(weight, rt[:, :, 9, :], rt[:, :, 10, :], ALU.add).then_inc(weight_ready, 1)

            pool.wait_ge(ffn_in, 16)
            for b in range(TB):
                pool.wait_ge(x2_ready, 2 * b + 1)
                nc.gpsimd.tensor_tensor(*scaled_half(b, 0), ALU.mult).then_inc(xg_pool, 1)
            pool.wait_ge(meansq, 2)
            nc.gpsimd.tensor_tensor(stat[:, 4:6], stat[:, 2:4], halfneg[:], ALU.pow).then_inc(rstd, 1)
            route_weights()
            for b in range(TB):
                pool.wait_ge(meansq, 3 + b)
                nc.gpsimd.tensor_tensor(stat[:, 4 + b:5 + b], stat[:, 2 + b:3 + b], halfneg[:, 0:1], ALU.pow).then_inc(rstd, 1)

        @block.scalar
        def _(act):
            steps = [0]

            def link(ins):
                steps[0] += 1
                ins.then_inc(act_step, 1)
                act.wait_ge(act_step, steps[0])

            for b in range(TB):
                act.dma_start(x_sb[:, b, :], x_in[0, b * P:(b + 1) * P, :]).then_inc(x_in_s[b], 16)

            for b in range(TB):
                act.wait_ge(x_in_s[b], 16)
                if b:
                    act.wait_ge(sumsq, b)
                nc.scalar.activation(hT[:, 0:4, :].rearrange("p k t -> p (k t)"), x_sb[:, b, :], ACT.Square, accum_out=stat[:, b:b + 1]).then_inc(sumsq, 1)
            act.wait_ge(cols_psum, 1)
            nc.scalar.activation(cols[:, FIRST_ROWS], bank[0][:, FIRST_ROWS], ACT.Copy).then_inc(cols_ready, 1)
            for g in range(2):
                ins = nc.scalar.activation(s5c[64 * g:64 * g + 64, 0, :],
                                           bank[0][64 * g:64 * g + 64, 128 + g:128 + GROUPS:2], ACT.Copy)
            ins.then_inc(cols_ready, 1)
            act.wait_ge(cols_ready, 2)
            for k in EVEN_BANKS:
                act.wait_ge(hT_psum, k - k % 2 + 2)
                nc.scalar.activation(hT[:, k, :], psum_half(8 + k), ACT.Copy,
                                     scale=cols[:, R_GMIX + k:R_GMIX + k + 1]).then_inc(hT_act, 1)
            act.wait_ge(cols_psum, 2)
            nc.scalar.activation(cols[:, LATER_ROWS], bank[0][:, LATER_ROWS], ACT.Copy).then_inc(cols_ready, 1)
            act.wait_ge(angle_ready, 1)
            nc.scalar.activation(s5c[:, 5, :], s5c[:, 4, :], ACT.Sin)
            nc.scalar.activation(s5c[:, 6, :], s5c[:, 4, :], ACT.Sin, scale=0.5).then_inc(sines_ready, 1)
            for n in range(YB):
                act.wait_ge(u_psum, n - n % 2 + 2)
                nc.scalar.activation(uT[:, n, :], psum_half(4 + n), ACT.Copy).then_inc(u_ready, 1)
            act.wait_ge(bt_psum, 1)
            for i in range(2):
                ins = nc.scalar.activation(BT[:, :, i, :], bank[4 + i][:].rearrange("p (b n) -> p b n", b=YB), ACT.Copy)
            ins.then_inc(bt_ready, 1)

            def main(g):
                if g < 24:
                    j = g // 3
                    if g % 3 == 0:
                        act.wait_ge(xbc_psum, g + 1)
                        if j >= 2:
                            act.wait_ge(z_ready, j - 1)
                        nc.scalar.activation(xs[:, j % 2, :], bank[2 * (j % 2)][:, 0:T], ACT.Copy).then_inc(xs_ready, 1)
                elif g < 32:
                    n = g - 24
                    act.wait_ge(ya_psum, n + 1)
                    nc.scalar.activation(mixed[:, n, :], bank[n % 4][:, 0:T], ACT.Copy).then_inc(ya_ready, 1)
                elif g < 40:
                    n = g - 32
                    act.wait_ge(ga_psum, n + 1)
                    if n >= 2:
                        act.wait_ge(ga_used, n - 1)
                    nc.scalar.activation(gate[:, n % 2, :], bank[n % 4][:, 0:T], ACT.Sigmoid,
                                         bias=cols[:, R_GATEB + n:R_GATEB + n + 1]).then_inc(ga_ready, 1)
                else:
                    n = g - 40
                    act.wait_ge(gb_psum, n + 1)
                    nc.scalar.activation(z_sb[:, n, :], bank[n % 4][:, 0:T], ACT.Sigmoid,
                                         bias=cols[:, R_GATEB + KD + n:R_GATEB + KD + n + 1]).then_inc(gb_ready, 1)

            def s5(t):
                if t >= 6 and (t - 6) % 4 == 0:
                    gelu((t - 6) // 4)
                if t == ST + S5_LAG - 1:
                    gelu(YB - 1)

            def gelu(b):
                act.wait_ge(ypre_ready, b + 1)
                nc.scalar.activation(yT[:, b, :], yT[:, b, :], ACT.Gelu_apprx_tanh).then_inc(y_ready, 1)

            for what, n in SCHEDULE:
                main(n) if what == "main" else s5(n)
            act.wait_ge(s_ready, ST)
            act.wait_ge(rot_ready, YB)
            for b in range(TB):
                act.dma_start(x_sb[:, b, :], x_in[0, b * P:(b + 1) * P, :]).then_inc(x_in_s[b], 16)
            act.dma_start(g_ffn, norm_ffn.to_broadcast([P, D])).then_inc(ffn_in, 16)
            act.wait_ge(ga_used, KD)
            for n in range(KD):
                act.wait_ge(glu_psum, 2 * n + 1)
                if n >= 2:
                    act.wait_ge(mixed_ready, n - 1)
                nc.scalar.activation(gate[:, n % 2, :], bank[2 * (n % 2)][:, 0:T], ACT.Sigmoid).then_inc(glu_sig, 1)
            act.wait_ge(glu_psum, 2 * KD)
            act.dma_start(g_fin, norm_final.unsqueeze(0).to_broadcast([P, D])).then_inc(fin_in, 16)
            for b in range(TB):
                act.wait_ge(x2_ready, 2 * (b + 1))
                act.wait_ge(sumsq, 2 + b)
                nc.scalar.activation(y_sb, x_sb[:, b, :], ACT.Square, accum_out=stat[:, b:b + 1]).then_inc(sumsq, 1)
            for k in EVEN_BANKS:
                act.wait_ge(h2T_psum, k - k % 2 + 2)
                nc.scalar.activation(hT[:, k, :], psum_half(8 + k), ACT.Copy).then_inc(hT_act, 1)
            act.wait_ge(h2T_psum, KD)
            act.wait_ge(rstd, 2)
            for b in range(TB):
                nc.scalar.activation(h2[:, b], h2[:, b], ACT.Copy, scale=stat[:, 4 + b:5 + b]).then_inc(h2_ready, 1)
            for n in range(2):
                act.wait_ge(expin_ready, n + 1)
                if n == 0:
                    ins = nc.scalar.activation(rt[:, :, 1, 0:NEG], rt[:, :, 0, 0:NEG], ACT.Exp)
                else:
                    ins = nc.scalar.activation(rs[:, 9, :], rs[:, 8, :], ACT.Exp)
                ins.then_inc(exp_ready, 1)

            def experts(rnd):
                with act.Fori(0, BODIES) as it:
                    for pk in range(BODY_PACKS):
                        done = rnd * PACKS + it * BODY_PACKS + (pk + 1)
                        for part in range(2):
                            if part == 1:
                                act.wait_ge(wselT_psum, done)
                                nc.scalar.activation(wselT, bank[5][:, 0:TB * P].rearrange("p (b t) -> p b t", b=TB),
                                                     ACT.Copy).then_inc(wselT_ready, 1)
                            act.wait_ge(gather_psum, done * 3 - 2 + part)
                            nc.scalar.activation(*gathered(part), ACT.Copy).then_inc(xT_act, 1)
                        act.wait_ge(up_psum, done)
                        nc.scalar.activation(silu, bank[4][:], ACT.Silu).then_inc(silu_ready, 1)
                        act.wait_ge(actT_psum, done)
                        nc.scalar.activation(actT, bank[4][:].rearrange("p (c s) -> p c s", c=KF),
                                             ACT.Copy).then_inc(actT_ready, 1)
                        act.wait_ge(down_psum, done * 2 - 1)
                        nc.scalar.activation(y_sb[:, 0:512], bank[6][:], ACT.Copy).then_inc(y_act, 1)

            experts(0)
            act.wait_ge(most_ready, 1)
            most_r = act.value_load(most[0:1, 0:1], min_val=0, max_val=T)
            with act.If(most_r > SLOTS):
                with act.Fori(1, ROUNDS) as rnd:
                    with act.If(most_r > rnd * SLOTS):
                        experts(rnd)
            act.wait_ge(moe_psum, 1)
            for b in range(TB):
                for h in range(2):
                    i = 2 * b + h
                    if b == 1:
                        act.wait_ge(fg_ready, h + 1)
                    nc.scalar.activation(h2[:, b, 4 * h:4 * h + 4, :].rearrange("p k n -> p (k n)"), bank[i][:],
                                         ACT.Square, accum_out=stat[:, 6 + i:7 + i]).then_inc(sumsq, 1)
            act.wait_ge(rstd, 4)
            nc.scalar.activation(x_sb[:, 1, 0:512], x_sb[:, 1, 0:512], ACT.Copy, scale=stat[:, 5:6]).then_inc(out_act, 1)

        @block.vector
        def _(dve):
            steps = [0]

            def link(ins):
                steps[0] += 1
                ins.then_inc(dve_step, 1)
                dve.wait_ge(dve_step, steps[0])

            V = nc.vector

            def mean_square():
                V.tensor_scalar(stat[:, 2:4], stat[:, 0:2], 1.0 / D, EPS, ALU.mult, ALU.add).then_inc(meansq, 1)

            def row_mean(b):
                link(V.tensor_tensor(stat[:, b:b + 1], stat[:, 6 + 2 * b:7 + 2 * b], stat[:, 7 + 2 * b:8 + 2 * b], ALU.add))
                V.tensor_scalar(stat[:, 2 + b:3 + b], stat[:, b:b + 1], 1.0 / D, EPS, ALU.mult, ALU.add).then_inc(meansq, 1)

            dve.wait_ge(sumsq, 2)
            mean_square()
            dve.wait_ge(rstd, 1)
            for b in range(TB):
                V.tensor_scalar(xn[:, b, :], x_sb[:, b, :], stat[:, 4 + b:5 + b], None, ALU.mult).then_inc(xn_ready, 1)
            dve.wait_ge(cols_ready, 2)
            dve.wait_ge(dt_ready, 1)
            are, aim = cols[:, R_ARE:R_ARE + ST], cols[:, R_AIM:R_AIM + ST]

            def c(i):
                return s5c[:, i, :]

            V.tensor_tensor(c(1), are, dt_t[:], ALU.mult).then_inc(expo_ready, 1)
            link(V.tensor_tensor(c(3), aim, dt_t[:], ALU.mult))
            link(V.tensor_scalar(c(7), c(3), 1.0 / TWO_PI, ROUNDER, ALU.mult, ALU.add))
            link(V.tensor_scalar(c(7), c(7), ROUNDER, None, ALU.subtract))
            for part in (PI_HI, PI_MID, PI_LO):
                link(V.scalar_tensor_tensor(c(3), c(7), -part, c(3), ALU.mult, ALU.add))
            V.tensor_scalar(c(4), c(3), PI_CLAMP, -PI_CLAMP, ALU.min, ALU.max).then_inc(angle_ready, 1)
            for k in ODD_BANKS:
                dve.wait_ge(hT_psum, k - k % 2 + 2)
                V.tensor_scalar(hT[:, k, :], psum_half(8 + k), cols[:, R_GMIX + k:R_GMIX + k + 1], None, ALU.mult)\
                    .then_inc(hT_dve, 1)
            dve.wait_ge(consts, 2)
            link(V.tensor_scalar(par_i[:], par_i[:], 4, 1, ALU.logical_shift_right, ALU.bitwise_and))
            link(V.tensor_copy(par[:, 1:2], par_i[:]))
            link(V.tensor_scalar(par[:, 0:1], par[:, 1:2], -1.0, 1.0, ALU.mult, ALU.add))
            dve.wait_ge(c_in, 32)
            for i in range(2):
                for g in range(2):
                    ins = V.tensor_scalar(zc[:, i, :, g, :], cld[:, i], par[:, g:g + 1], None, ALU.mult)
            ins.then_inc(zc_ready, 1)
            link(V.tensor_tensor(c(8), are, are, ALU.mult))
            link(V.tensor_tensor(c(9), aim, aim, ALU.mult))
            link(V.tensor_tensor(c(8), c(8), c(9), ALU.add))
            link(V.reciprocal(c(9), c(8)))
            dve.wait_ge(sines_ready, 1)
            link(V.tensor_tensor(c(6), c(6), c(6), ALU.mult))
            link(V.tensor_scalar(c(6), c(6), -2.0, 1.0, ALU.mult, ALU.add))
            dve.wait_ge(rho_ready, 1)
            link(V.tensor_tensor(c(10), c(2), c(6), ALU.mult))
            link(V.tensor_scalar(c(10), c(10), 1.0, None, ALU.subtract))
            link(V.tensor_tensor(c(11), c(2), c(5), ALU.mult))
            V.tensor_tensor(c(12), c(10), are, ALU.mult)
            link(V.tensor_tensor(c(13), c(11), aim, ALU.mult))
            link(V.tensor_tensor(c(12), c(12), c(13), ALU.add))
            link(V.tensor_tensor(c(14), c(12), c(9), ALU.mult))
            V.tensor_tensor(c(12), c(11), are, ALU.mult)
            link(V.tensor_tensor(c(13), c(10), aim, ALU.mult))
            link(V.tensor_tensor(c(12), c(12), c(13), ALU.subtract))
            link(V.tensor_tensor(c(15), c(12), c(9), ALU.mult))
            dve.wait_ge(b_in, 32)
            kr = c(14).unsqueeze(2).to_broadcast([P, ST, GH])
            ki = c(15).unsqueeze(2).to_broadcast([P, ST, GH])
            V.tensor_tensor(btmp[:, 0], bld[:, 0], kr, ALU.mult)
            V.tensor_tensor(btmp[:, 1], bld[:, 1], ki, ALU.mult)
            V.tensor_tensor(btmp[:, 2], bld[:, 1], kr, ALU.mult)
            link(V.tensor_tensor(btmp[:, 3], bld[:, 0], ki, ALU.mult))
            for g in range(2):
                h = slice(64 * g, 64 * g + 64)
                V.tensor_tensor(zb[h, 0, :, GH * g:GH * g + GH], btmp[h, 0], btmp[h, 1], ALU.subtract)
                ins = V.tensor_tensor(zb[h, 1, :, GH * g:GH * g + GH], btmp[h, 2], btmp[h, 3], ALU.add)
            ins.then_inc(zb_ready, 1)

            def power(i, k, tbl):
                return tbl[:, i, :, k:k + 1]

            for tbl, first in ((lowT, None), (highT, lowT)):
                if first is None:
                    V.tensor_copy(power(0, 1, tbl), c(6).unsqueeze(2))
                    link(V.tensor_copy(power(1, 1, tbl), c(5).unsqueeze(2)))
                else:
                    r8, i8 = power(0, 8, first), power(1, 8, first)
                    V.tensor_tensor(ptmp[:, 0, :, 0:1], r8, r8, ALU.mult)
                    V.tensor_tensor(ptmp[:, 1, :, 0:1], i8, i8, ALU.mult)
                    link(V.scalar_tensor_tensor(power(1, 1, tbl), r8, 2.0, i8, ALU.mult, ALU.mult))
                    link(V.tensor_tensor(power(0, 1, tbl), ptmp[:, 0, :, 0:1], ptmp[:, 1, :, 0:1], ALU.subtract))
                n = 1
                while n < 16:
                    if n > 1:
                        r, i = power(0, n // 2, tbl), power(1, n // 2, tbl)
                        V.tensor_tensor(ptmp[:, 0, :, 0:1], r, r, ALU.mult)
                        V.tensor_tensor(ptmp[:, 1, :, 0:1], i, i, ALU.mult)
                        link(V.scalar_tensor_tensor(power(1, n, tbl), r, 2.0, i, ALU.mult, ALU.mult))
                        link(V.tensor_tensor(power(0, n, tbl), ptmp[:, 0, :, 0:1], ptmp[:, 1, :, 0:1], ALU.subtract))
                        m = n - 1
                        lo_r, lo_i = tbl[:, 0, :, 1:n], tbl[:, 1, :, 1:n]
                        pr = power(0, n, tbl).to_broadcast([P, ST, m])
                        pi = power(1, n, tbl).to_broadcast([P, ST, m])
                        t0, t1 = ptmp[:, 0, :, 0:m], ptmp[:, 1, :, 0:m]
                        V.tensor_tensor(t0, lo_r, pr, ALU.mult)
                        link(V.tensor_tensor(t1, lo_i, pi, ALU.mult))
                        link(V.tensor_tensor(tbl[:, 0, :, n + 1:2 * n], t0, t1, ALU.subtract))
                        V.tensor_tensor(t0, lo_r, pi, ALU.mult)
                        link(V.tensor_tensor(t1, lo_i, pr, ALU.mult))
                        link(V.tensor_tensor(tbl[:, 1, :, n + 1:2 * n], t0, t1, ALU.add))
                    n *= 2
            V.tensor_copy(par[:, 0:1], par[:, 1:2]).then_inc(powers_ready, 1)
            dve.wait_ge(bt_psum, 2)
            for i, (src, scale) in enumerate(((6, 1.0), (7, -1.0))):
                ins = V.tensor_scalar(CT[:, i], bank[src][:].rearrange("p (b n) -> p b n", b=YB), scale, None, ALU.mult)
            ins.then_inc(ct_ready, 1)

            def conv(j):
                s = j % 2
                w = [cols[:, R_CONVW + KD * i + j:R_CONVW + KD * i + j + 1] for i in range(3)]
                dve.wait_ge(xs_ready, j + 1)
                dve.wait_ge(xbc_psum, 3 * j + 3)
                link(V.tensor_tensor(v_sb[:, s, 2:T + 2], bank[2 * s + 1][:, T:2 * T], xs[:, s, :], ALU.mult))
                link(V.tensor_scalar(ct[:, 0, :], v_sb[:, s, 2:T + 2], w[2], cols[:, R_CONVB + j:R_CONVB + j + 1],
                                     ALU.mult, ALU.add))
                link(V.scalar_tensor_tensor(ct[:, 1, :], v_sb[:, s, 1:T + 1], w[1], ct[:, 0, :], ALU.mult, ALU.add))
                link(V.scalar_tensor_tensor(ct[:, 0, :], v_sb[:, s, 0:T], w[0], ct[:, 1, :], ALU.mult, ALU.add))
                V.tensor_tensor(z_sb[:, j, :], bank[2 * s + 1][:, 0:T], ct[:, 0, :], ALU.mult).then_inc(z_ready, 1)
                dve.wait_ge(z_ready, j + 1)

            def s5_step(t):
                b, q = t // 4, t % 4
                cos, sin = rot[:, b % 2, 0, q, :], rot[:, b % 2, 1, q, :]
                if q == 0:
                    dve.wait_ge(rot_ready, b + 1)
                dve.wait_ge(bu_psum, t + 1)
                bu = bank[4 + t % 2][:].rearrange("p (i t) -> p i t", i=2)
                cos2, sin2 = (w.unsqueeze(1).to_broadcast([P, 2, T]) for w in (cos, sin))
                V.tensor_tensor(turned[:, 0], bu, cos2, ALU.mult)
                V.tensor_tensor(turned[:, 1], bu, sin2, ALU.mult).then_inc(bu_used, 1)
                dve.wait_ge(bu_used, t + 1)
                zin, zst = turned[:, 0], turned[:, 1]
                V.tensor_tensor(zin[:, 0, :], turned[:, 0, 0, :], turned[:, 1, 1, :], ALU.add)
                link(V.tensor_tensor(zin[:, 1, :], turned[:, 0, 1, :], turned[:, 1, 0, :], ALU.subtract))
                rho = s5c[:, 2, t:t + 1].to_broadcast([P, T])
                V.tensor_tensor_scan(zst[:, 0, :], rho, zin[:, 0, :], 0.0, ALU.mult, ALU.add)
                link(V.tensor_tensor_scan(zst[:, 1, :], rho, zin[:, 1, :], 0.0, ALU.mult, ALU.add))
                if t >= 2:
                    dve.wait_ge(s_ready, t - 1)
                if t >= 4:
                    dve.wait_ge(q_used, t - t % 2 - 2)
                V.tensor_tensor(s_sb[:, t % 4], zst, cos2, ALU.mult)
                ins = V.tensor_tensor(sprod[:, t % 2], zst, sin2, ALU.mult)
                ins.then_inc(q_ready, 1)
                dve.wait_ge(q_ready, t + 1)
                if q == 3:
                    V.tensor_copy(par[:, 0:1], par[:, 1:2]).then_inc(rot_used, 1)
                    dve.wait_ge(rot_used, b + 1)

            def y_pre(b):
                dve.wait_ge(q_used, 4 * b + 4)
                V.scalar_tensor_tensor(yT[:, b, :], uT[:, b, :], cols[:, R_SSMD + b:R_SSMD + b + 1],
                                       bank[6 + b % 2][:, 0:T], ALU.mult, ALU.add).then_inc(ypre_ready, 1)

            def main(g):
                if g < 24 and g % 3 == 2:
                    conv(g // 3)
                elif 32 <= g < 40:
                    n = g - 32
                    dve.wait_ge(ga_ready, n + 1)
                    V.tensor_tensor(mixed[:, n, :], mixed[:, n, :], gate[:, n % 2, :], ALU.mult).then_inc(ga_used, 1)

            def s5(t):
                if t < ST:
                    s5_step(t)
                if t >= 6 and (t - 6) % 4 == 0:
                    y_pre((t - 6) // 4)
                if t == ST + S5_LAG - 1:
                    y_pre(YB - 1)

            for what, n in SCHEDULE:
                main(n) if what == "main" else s5(n)
            dve.wait_ge(gb_ready, KD)
            dve.wait_ge(ga_used, KD)
            for n in range(KD):
                dve.wait_ge(glu_sig, n + 1)
                dve.wait_ge(glu_psum, 2 * n + 2)
                link(V.tensor_tensor(xs[:, 0, :], bank[2 * (n % 2) + 1][:, 0:T], gate[:, n % 2, :], ALU.mult))
                link(V.tensor_tensor(xs[:, 1, :], xs[:, 0, :], z_sb[:, n, :], ALU.mult))
                V.tensor_tensor(mixed[:, n, :], mixed[:, n, :], xs[:, 1, :], ALU.add).then_inc(mixed_ready, 1)
                dve.wait_ge(mixed_ready, n + 1)
            dve.wait_ge(ffn_in, 16)
            for b in range(TB):
                dve.wait_ge(x_in_s[b], 32)
                for h in range(2):
                    xs_h = x_sb[:, b, 512 * h:512 * h + 512]
                    dve.wait_ge(wo_psum, 2 * b + h + 1)
                    V.tensor_tensor(xs_h, bank[4 + 2 * b + h][:], xs_h, ALU.add).then_inc(x2_ready, 1)
                dve.wait_ge(x2_ready, 2 * b + 2)
                V.tensor_tensor(*scaled_half(b, 1), ALU.mult).then_inc(xg_dve, 1)
            dve.wait_ge(sumsq, 4)
            mean_square()
            for k in ODD_BANKS:
                dve.wait_ge(h2T_psum, k - k % 2 + 2)
                V.tensor_copy(hT[:, k, :], psum_half(8 + k)).then_inc(hT_dve, 1)

            def per_token(ap, n):
                return ap.unsqueeze(2).to_broadcast([P, TB, n])

            def rcol(i, n=NE):
                return rt[:, :, i, 0:n]

            def first_of(values, best, n, tmp):
                for b in range(TB):
                    ins = V.scalar_tensor_tensor(tmp[:, b], values[:, b], rs[:, best, b:b + 1], from_end[:, NE - n:], ALU.is_equal, ALU.mult)
                link(ins)
                link(V.tensor_reduce(rs[:, 15, :], tmp, AX.X, ALU.max))

            def first_match(hot, values, best, n, tmp):
                first_of(values, best, n, tmp)
                link(V.tensor_tensor(hot, tmp, per_token(rs[:, 15, :], n), ALU.is_equal))

            dve.wait_ge(lgT_psum, 1)
            V.tensor_copy(lgT, bank[4][0:N_LOGITS, 0:T]).then_inc(lgT_ready, 1)
            dve.wait_ge(logits_psum, 1)
            dve.wait_ge(route_in, 64)
            logits = bank[4][:, T:T + TB * N_LOGITS].rearrange("p (b n) -> p b n", b=TB)
            dve.wait_ge(rstd, 2)
            for b in range(TB):
                r = stat[:, 4 + b:5 + b]
                ins = V.scalar_tensor_tensor(lg[:, b, :], logits[:, b, :], r, br[:], ALU.mult, ALU.add)
            link(ins)
            link(V.tensor_reduce(rs[:, 0, :], lg[:, :, 0:NEG], AX.X, ALU.max))
            V.tensor_tensor(rcol(0, NEG), lg[:, :, 0:NEG], per_token(rs[:, 0, :], NEG), ALU.subtract).then_inc(expin_ready, 1)
            first_of(lg[:, :, 0:NEG], 0, NEG, rcol(5, NEG))
            for b in range(TB):
                ins = V.tensor_scalar(rt[:, b, 4, 0:NEG], rt[:, b, 5, 0:NEG], rs[:, 15, b:b + 1], MASKED, ALU.not_equal, ALU.mult)
            link(ins)
            for b in range(TB):
                ins = V.tensor_tensor(rt[:, b, 6, :].rearrange("p (g e) -> p g e", g=NEG),
                                      lg[:, b, NEG:].rearrange("p (g e) -> p g e", g=NEG),
                                      rt[:, b, 4, 0:NEG].unsqueeze(2).to_broadcast([P, NEG, EG]), ALU.add)
            link(ins)
            link(V.tensor_reduce(rs[:, 1, :], rcol(6), AX.X, ALU.max))
            first_match(rcol(7), rcol(6), 1, NE, rcol(9))
            link(V.scalar_tensor_tensor(rcol(6), rcol(7), 3.0 * MASKED, rcol(6), ALU.mult, ALU.add))
            link(V.tensor_reduce(rs[:, 2, :], rcol(6), AX.X, ALU.max))
            V.tensor_tensor(rs[:, 8, :], rs[:, 2, :], rs[:, 1, :], ALU.subtract).then_inc(expin_ready, 1)
            first_match(rcol(8), rcol(6), 2, NE, rcol(9))
            V.tensor_tensor(member[:], rcol(7), rcol(8), ALU.add).then_inc(member_ready, 1)
            dve.wait_ge(exp_ready, 1)
            V.tensor_reduce(rs[:, 11, :], rcol(1, NEG), AX.X, ALU.add).then_inc(group_sum, 1)
            dve.wait_ge(member_ready, 1)
            link(V.tensor_scalar(rcol(11), member[:], -UNSELECTED, UNSELECTED, ALU.mult, ALU.add))
            dve.wait_ge(rank_psum, 1)
            V.tensor_tensor(rank, rcol(11), bank[5][:, 0:2 * NE].rearrange("p (b n) -> p b n", b=TB), ALU.add)
            link(V.tensor_reduce(cnt_f[:], bank[5][:, 2 * NE:3 * NE], AX.X, ALU.max))
            V.tensor_copy(most[:], cnt_f[:]).then_inc(most_ready, 1)

            def experts(rnd):
                with dve.Fori(0, BODIES) as it:
                    for pk in range(BODY_PACKS):
                        done = rnd * PACKS + it * BODY_PACKS + (pk + 1)
                        first = it * (BODY_PACKS * PACK) + pk * PACK
                        shape = [P, TB, PACK, SLOTS]
                        dve.wait_ge(slots_moved, rnd + 1)
                        V.tensor_tensor(sel, slot_no[:].unsqueeze(1).unsqueeze(1).to_broadcast(shape),
                                        rank[:, :, bass.ds(first, PACK)].unsqueeze(3).to_broadcast(shape),
                                        ALU.is_equal).then_inc(sel_ready, 1)
                        dve.wait_ge(sel_ready, done)
                        dve.wait_ge(weight_ready, 1)
                        V.tensor_tensor(wsel, sel,
                                        weight[:, :, bass.ds(first, PACK)].unsqueeze(3).to_broadcast(shape),
                                        ALU.mult).then_inc(wsel_ready, 1)
                        dve.wait_ge(gather_psum, done * 3)
                        V.tensor_copy(*gathered(2)).then_inc(xT_dve, 1)
                        dve.wait_ge(silu_ready, done)
                        dve.wait_ge(up_psum, done)
                        V.tensor_tensor(act_sb.rearrange("p c q -> p q c"),
                                        silu.rearrange("p (q c) -> p q c", c=KF),
                                        bank[5][:].rearrange("p (q c) -> p q c", c=KF), ALU.mult).then_inc(act_ready, 1)
                        dve.wait_ge(down_psum, done * 2)
                        V.tensor_copy(y_sb[:, 512:D], bank[7][:]).then_inc(y_dve, 1)
                V.tensor_scalar(slot_no[:], slot_no[:], float(SLOTS), None, ALU.add).then_inc(slots_moved, 1)

            experts(0)
            dve.wait_ge(most_ready, 1)
            most_r = dve.value_load(most[0:1, 0:1], min_val=0, max_val=T)
            with dve.If(most_r > SLOTS):
                with dve.Fori(1, ROUNDS) as rnd:
                    with dve.If(most_r > rnd * SLOTS):
                        experts(rnd)
            dve.wait_ge(moe_psum, 1)
            dve.wait_ge(fin_in, 16)
            for h in range(2):
                half = slice(512 * h, 512 * h + 512)
                V.tensor_tensor(x_sb[:, 1, half], bank[2 + h][:], g_fin[:, half], ALU.mult).then_inc(fg_ready, 1)
            dve.wait_ge(sumsq, 6)
            row_mean(0)
            dve.wait_ge(rstd, 3)
            for h in range(2):
                half = slice(512 * h, 512 * h + 512)
                V.scalar_tensor_tensor(x_sb[:, 0, half], bank[h][:], stat[:, 4:5], g_fin[:, half],
                                       ALU.mult, ALU.mult).then_inc(out_dve, 1)
                if h == 0:
                    dve.wait_ge(sumsq, 8)
                    row_mean(1)
            dve.wait_ge(rstd, 4)
            dve.wait_ge(fg_ready, 2)
            V.tensor_scalar(x_sb[:, 1, 512:], x_sb[:, 1, 512:], stat[:, 5:6], None, ALU.mult).then_inc(out_dve, 1)

        @block.tensor
        def _(pe):
            pe.sem_inc(expert_units, BODY_UNITS)
            MM = nc.tensor.matmul

            def keep_clock(to, n):
                for _ in range(n):
                    MM(bank[to][:, 0:P], ident[:], ident[:], start=True, stop=True)

            pe.wait_ge(consts, 1)
            keep_clock(1, 7)
            pe.wait_ge(rows_in, 16 * 4)
            nc.tensor.transpose(bank[0][:, FIRST_ROWS], rows[FIRST_ROWS, :], ident[FIRST_ROWS, FIRST_ROWS])
            MM(bank[0][:, 128:128 + GROUPS], ones[0:1, :], logdt_row[:], start=True, stop=True).then_inc(cols_psum, 1)
            keep_clock(1, 4)
            for b in range(TB):
                pe.wait_ge(xn_ready, b + 1)
                for k in range(KD):
                    ins = nc.tensor.transpose(psum_half(8 + k)[:, b * P:(b + 1) * P], xn[:, b, k * P:(k + 1) * P], ident[:])
                    if b == TB - 1:
                        ins.then_inc(hT_psum, 1)
            owed = [0]

            def project(dst, w, n, rhs, done, kn=KD, arrives=None):
                for k in range(kn):
                    if arrives is not None:
                        pe.wait_ge(arrives, k + 1)
                    ins = MM(dst, w[:, k, n * P:(n + 1) * P], rhs[:, k, :], start=k == 0, stop=k == kn - 1)
                    if k == 0 and owed[0]:
                        ins.then_inc(units_used, owed[0])
                        owed[0] = 0
                return ins.then_inc(done, 1)

            mix_loaded(pe, U_U)
            for i, k in enumerate(EVEN_BANKS + ODD_BANKS):
                pe.wait_ge(*((hT_act, i + 1) if i < 4 else (hT_dve, i - 3)))
                ins = MM(psum_half(4), w8(U_U)[:, k, 0:P], hT[:, k, :], start=i == 0, stop=i == KD - 1)
            ins.then_inc(u_psum, 1)
            pe.wait_ge(later_rows_in, 16 * 4)
            pe.wait_ge(cols_ready, 2)
            nc.tensor.transpose(bank[0][:, LATER_ROWS], rows[LATER_ROWS, :], ident[LATER_ROWS, LATER_ROWS]).then_inc(cols_psum, 1)
            for n in range(1, YB):
                project(psum_half(4 + n), w8(U_U), n, hT, u_psum)
            owed[0] += 1
            pe.wait_ge(zb_ready, 1)
            for i in range(2):
                for b in range(YB):
                    ins = nc.tensor.transpose(bank[4 + i][:, b * P:(b + 1) * P],
                                              zb[:, i, 4 * b:4 * b + 4, :].rearrange("p t h -> p (t h)"), ident[:])
            ins.then_inc(bt_psum, 1)
            pe.wait_ge(zc_ready, 1)
            for i in range(2):
                for b in range(YB):
                    ins = nc.tensor.transpose(bank[6 + i][:, b * P:(b + 1) * P],
                                              zc[:, i, b].rearrange("p g n -> p (g n)"), ident[:])
            ins.then_inc(bt_psum, 1)

            def main(g):
                if g < 24:
                    j, part = g // 3, g % 3
                    unit = U_XBC + 3 * (j // 4) + part
                    if g == 0:
                        pe.wait_ge(cols_ready, 3)
                    if g == 3:
                        pe.wait_ge(u_ready, YB)
                    if part == 0 and j >= 2:
                        pe.wait_ge(z_ready, j - 1)
                    mix_loaded(pe, unit)
                    s = 2 * (j % 2)
                    dst = (bank[s][:, 0:T], bank[s + 1][:, 0:T], bank[s + 1][:, T:2 * T])[part]
                    project(dst, w8(unit), j % 4, hT, xbc_psum)
                elif g < 32:
                    n = g - 24
                    if n <= 1:
                        pe.wait_ge(z_ready, KD - 1 + n)
                    if n >= 4:
                        pe.wait_ge(ya_ready, n - 3)
                    mix_loaded(pe, U_CO + n // 4)
                    project(bank[n % 4][:, 0:T], w8(U_CO + n // 4), n % 4, z_sb, ya_psum, arrives=z_ready if n == 0 else None)
                elif g < 40:
                    n = g - 32
                    pe.wait_ge(*((ya_ready, n + 5) if n < 4 else (ga_ready, n - 3)))
                    mix_loaded(pe, U_GA + n // 4)
                    project(bank[n % 4][:, 0:T], w8(U_GA + n // 4), n % 4, hT, ga_psum)
                else:
                    n = g - 40
                    pe.wait_ge(*((ga_ready, n + 5) if n < 4 else (gb_ready, n - 3)))
                    mix_loaded(pe, U_GB + n // 4)
                    project(bank[n % 4][:, 0:T], w8(U_GB + n // 4), n % 4, hT, gb_psum)
                if g in (11, 23):
                    owed[0] += 3
                if g >= 24 and g % 4 == 3:
                    owed[0] += 1

            def s5(t):
                if t < ST and t % 2 == 0:
                    b, q = t // 4, t % 4
                    if t == 0:
                        pe.wait_ge(bt_ready, 1)
                        pe.wait_ge(u_ready, YB)
                    if t >= 2:
                        pe.wait_ge(bu_used, t)
                    for i in range(2):
                        for n in range(2):
                            r = slice(32 * (q + n), 32 * (q + n) + 32)
                            ins = MM(bank[4 + n][:, i * T:(i + 1) * T], BT[r, b, i, :], uT[r, b, :],
                                     start=True, stop=True)
                    ins.then_inc(bu_psum, 2)
                if t > S5_LAG and t % 2:
                    t -= S5_LAG + 1
                    b, q = t // 4, t % 4
                    if t == 0:
                        pe.wait_ge(ct_ready, 1)
                    if q == 0 and b >= 2:
                        pe.wait_ge(ypre_ready, b - 1)
                    pe.wait_ge(s_ready, t + 2)
                    for i in range(2):
                        for n in range(2):
                            c = slice(32 * (q + n), 32 * (q + n) + 32)
                            ins = MM(bank[6 + b % 2][c, 0:T], CT[:, i, b, c], s_sb[:, (t + n) % 4, i, :],
                                     start=i == 0, stop=i == 1)
                    ins.then_inc(q_used, 2)

            for what, n in SCHEDULE:
                main(n) if what == "main" else s5(n)

            def project_out(k):
                pe.wait_ge(mixed_ready, k + 1)
                mix_loaded(pe, U_WO[k // 4])
                for b in range(TB):
                    for h in range(2):
                        ins = MM(bank[4 + 2 * b + h][:], mixed[:, k, b * P:(b + 1) * P],
                                 w4(U_WO[k // 4])[:, k % 4, 512 * h:512 * h + 512], start=k == 0, stop=k == KD - 1)
                        if k == KD - 1:
                            ins.then_inc(wo_psum, 1)

            pe.wait_ge(y_ready, YB)
            pe.wait_ge(gb_ready, KD)
            for n in range(KD):
                if n >= 2:
                    pe.wait_ge(mixed_ready, n - 1)
                mix_loaded(pe, U_GLU[n // 4])
                for i in range(2):
                    project(bank[2 * (n % 2) + i][:, 0:T], glu_half(U_GLU[n // 4])[:, i], n % 4, yT, glu_psum, YB)
                if n == 3:
                    owed[0] += 1
                if n == KD - 1:
                    pe.wait_ge(glu_psum, 2 * KD)
                    pe.sem_inc(units_used, 1)
                if n >= 1:
                    project_out(n - 1)
                if n == 4:
                    owed[0] += 1
            project_out(KD - 1)
            pe.wait_ge(wo_psum, 2 * TB)
            pe.sem_inc(units_used, 1)

            for b in range(TB):
                pe.wait_ge(xg_pool, b + 1)
                pe.wait_ge(xg_dve, b + 1)
                for k in range(KD):
                    if b == 0 and k % 2 == 0:
                        pe.wait_ge(x2_ready, k // 2 + 1)
                    ins = nc.tensor.transpose(psum_half(8 + k)[:, b * P:(b + 1) * P], h2[:, b, k, :], ident[:])
                    if b == TB - 1:
                        ins.then_inc(h2T_psum, 1)
            pe.wait_ge(route_in, 64)
            for k in range(KD):
                if k in EVEN_BANKS:
                    pe.wait_ge(hT_act, 4 + max(2, EVEN_BANKS.index(k) + 1))
                else:
                    pe.wait_ge(hT_dve, 4 + ODD_BANKS.index(k) + 1)
                ins = MM(bank[4][0:N_LOGITS, 0:T], wr[:, k, :], hT[:, k, :], start=k == 0, stop=k == KD - 1)
            ins.then_inc(lgT_psum, 1)
            for b in range(TB):
                for h in range(2):
                    ins = MM(bank[2 * b + h][:], ident[:], x_sb[:, b, 512 * h:512 * h + 512], start=True, stop=True)
                    if (b, h) == (0, 0):
                        pe.wait_ge(lgT_ready, 1)
                        for c in range(TB):
                            ins = nc.tensor.transpose(bank[4][:, T + c * N_LOGITS:T + (c + 1) * N_LOGITS],
                                                      lgT[:, c * P:(c + 1) * P], ident[0:N_LOGITS, 0:N_LOGITS])
                        ins.then_inc(logits_psum, 1)
            ins.then_inc(residual_psum, 1)
            keep_clock(7, 14)
            pe.wait_ge(member_ready, 1)
            MM(bank[5][:, 0:NE], upper16[:], member[:, 0, :], start=True, stop=True)
            MM(bank[5][:, NE:2 * NE], ones16[:], member[:, 0, :], start=True, stop=False)
            MM(bank[5][:, NE:2 * NE], upper16[:], member[:, 1, :], start=False, stop=True)
            MM(bank[5][:, 2 * NE:3 * NE], ones16[:], member[:, 0, :], start=True, stop=False)
            MM(bank[5][:, 2 * NE:3 * NE], ones16[:], member[:, 1, :], start=False, stop=True).then_inc(rank_psum, 1)
            keep_clock(7, 7)

            def experts(rnd):
                with pe.Fori(0, BODIES) as it:
                    for pk in range(BODY_PACKS):
                        expert_pack(rnd, it, pk)

            def expert_pack(rnd, it, pk):
                done = rnd * PACKS + it * BODY_PACKS + (pk + 1)

                def unit(w):
                    v = pk * PACK_UNITS + w
                    slot = SLOT_OF[v]
                    dst, landed = slots[slot]
                    fills = (rnd * BODIES + it) * SLOT_OF.count(slot) + (transfers_to(slot, range(MIX_UNITS)) + SLOT_OF[:v + 1].count(slot))
                    pe.wait_ge(landed, fills * 16)
                    return dst.rearrange("p (e n) -> p e n", e=PACK)

                pe.wait_ge(sel_ready, done)
                if pk == 0:
                    pe.wait_ge(h2_ready, TB)
                def gather(ks):
                    for k in ks:
                        part = GATHER_PARTS.index(next(p for p in GATHER_PARTS if k in p))
                        at = (k - GATHER_PARTS[part][0]) * P
                        for b in range(TB):
                            ins = MM(bank[GATHER_BANKS[part]][:, at:at + P], h2[:, b, k, :],
                                     sel[:, b].rearrange("p e s -> p (e s)"), start=b == 0, stop=b == TB - 1)
                        if k == GATHER_PARTS[part][-1]:
                            ins.then_inc(gather_psum, 1)

                gather((0, 1))
                pe.wait_ge(wsel_ready, done)
                for b in range(TB):
                    ins = nc.tensor.transpose(bank[5][:, b * P:(b + 1) * P],
                                              wsel[:, b].rearrange("p e s -> p (e s)"), ident[:])
                ins.then_inc(wselT_psum, 1)
                gather((2,))
                pe.wait_ge(xT_act, done * 2 - 1)
                for w in range(8):
                    if w == 1:
                        gather((3, 4, 5, 6, 7))
                        pe.wait_ge(wselT_ready, done)
                    if w == 2:
                        pe.wait_ge(xT_act, done * 2)
                    if w == 4:
                        pe.wait_ge(xT_dve, done)
                    wt = unit(w)
                    for kk in range(2):
                        k = 2 * (w // 2) + kk
                        for e in range(PACK):
                            q = slice(SLOTS * e, SLOTS * e + SLOTS)
                            ins = MM(bank[4 + w % 2][q, :], xT[:, k, q], wt[:, e, 512 * kk:512 * kk + 512],
                                     start=k == 0, stop=k == KD - 1)
                    if w < 7:
                        ins.then_inc(expert_units, 1)
                    else:
                        ins.then_inc(up_psum, 1)
                pe.wait_ge(up_psum, done)
                pe.sem_inc(expert_units, 1)
                pe.wait_ge(act_ready, done)
                for c in range(KF):
                    ins = nc.tensor.transpose(bank[4][:, c * P:(c + 1) * P], act_sb[:, c, :], ident[:])
                ins.then_inc(actT_psum, 1)
                pe.wait_ge(actT_ready, done)
                for c in range(KF):
                    if c:
                        keep_clock(4, 9)
                    wt = unit(8 + c)
                    for h in range(2):
                        for e in range(PACK):
                            q = slice(SLOTS * e, SLOTS * e + SLOTS)
                            ins = MM(bank[6 + h][q, :], actT[:, c, q], wt[:, e, 512 * h:512 * h + 512],
                                     start=c == 0, stop=c == KF - 1)
                        if c == KF - 1:
                            ins.then_inc(down_psum, 1)
                    if c < KF - 1:
                        ins.then_inc(expert_units, 1)
                pe.wait_ge(down_psum, done * 2)
                pe.sem_inc(expert_units, 1)
                for h in range(2):
                    pe.wait_ge((y_act, y_dve)[h], done)
                    for b in range(TB):
                        MM(bank[2 * b + h][:], wselT[:, b, :], y_sb[:, 512 * h:512 * h + 512],
                           start=False, stop=True, skip_group_check=True)

            experts(0)
            pe.wait_ge(most_ready, 1)
            most_r = pe.value_load(most[0:1, 0:1], min_val=0, max_val=T)
            with pe.If(most_r > SLOTS):
                with pe.Fori(1, ROUNDS) as rnd:
                    with pe.If(most_r > rnd * SLOTS):
                        experts(rnd)
            MM(bank[4][:, 0:4], ident[:], ident[:, 0:4], start=True, stop=True).then_inc(moe_psum, 1)


_INS = ["x", "norm_mix", "w_in", "conv_w", "conv_b", "w_conv_out", "ssm_a_re", "ssm_a_im", "ssm_log_dt",
        "ssm_b_re", "ssm_b_im", "ssm_c_re", "ssm_c_im", "ssm_d", "w_glu_a", "w_glu_b", "gate_bias", "w_o",
        "norm_ffn", "w_route_group", "b_route_group", "w_route_expert", "b_route_expert", "w_gate", "w_up",
        "w_down", "norm_final"]


def kernel(**inputs):
    import numpy as np
    import concourse.bacc as bacc
    from concourse.bass_utils import run_bass_kernel_spmd

    nc = bacc.Bacc("TRN2", target_bir_lowering=False, num_devices=1, dynamic_dma_scratch_size=1024)
    arrays, args = {}, []
    for name in _INS:
        a = np.ascontiguousarray(inputs[name])
        arrays[f"in_{name}"] = a
        args.append(nc.dram_tensor(f"in_{name}", a.shape, mybir.dt.from_np(a.dtype), kind="ExternalInput").ap())
    args.append(nc.dram_tensor("out_dram", (1, T, D), mybir.dt.float32, kind="ExternalOutput").ap())
    block_kernel(nc, *args)
    r = run_bass_kernel_spmd(nc, [arrays], core_ids=[0])
    return r.results[0]["out_dram"]
```
